# Optimizing a Trainium2 kernel written in Bass

```python
import math
import jax, jax.numpy as jnp
from jax import lax
import numpy as np

D_MODEL = 1024
BATCH = 1
SEQ = 512
DEPTH = 1
DEC_BATCH = 8
DEC_SEQ = 16
PAST_LEN = 256

CHUNK = 64
D_CONV = D_MODEL
CONV_A_WIDTH = 31
SSM_EXPAND = 2
D_INNER = SSM_EXPAND * D_MODEL
SSM_HEAD_DIM = 64
N_SSM_HEADS = D_INNER // SSM_HEAD_DIM
N_GROUPS = 4
D_STATE = 128
CONV_B_WIDTH = 4
D_XBC = D_INNER + 2 * N_GROUPS * D_STATE
D_FF = 2816
N_BRANCHES = 2
SPLIT_IDX = (2 * D_CONV,
             2 * D_CONV + D_INNER,
             2 * D_CONV + D_INNER + D_XBC,
             2 * D_CONV + D_INNER + D_XBC + N_SSM_HEADS)
D_IN_PROJ = SPLIT_IDX[3] + N_BRANCHES * D_MODEL
RMS_EPS = 1e-6
LN_EPS = 1e-5
FFN_RES_WEIGHT = 0.5

kernel_name = "hybrid_conformer_mamba2_stream_step"

def rms_norm(x, g):
    xf = x.astype(jnp.float32)
    y = xf * lax.rsqrt(jnp.mean(xf * xf, axis=-1, keepdims=True) + RMS_EPS)
    return (y * g.astype(jnp.float32)).astype(x.dtype)

def layer_norm(x, g, b):
    xf = x.astype(jnp.float32)
    mu = jnp.mean(xf, axis=-1, keepdims=True)
    xc = xf - mu
    y = xc * lax.rsqrt(jnp.mean(xc * xc, axis=-1, keepdims=True) + LN_EPS)
    return (y * g.astype(jnp.float32) + b.astype(jnp.float32)).astype(x.dtype)

def swiglu_ffn(x, w_gate, w_up, w_down):
    return (jax.nn.silu(x @ w_gate) * (x @ w_up)) @ w_down

def causal_depthwise_conv(u, buf, w, b):
    k = w.shape[0]
    ext = jnp.concatenate([buf.astype(u.dtype), u], axis=1)
    out = lax.conv_general_dilated(ext, w[:, None, :].astype(u.dtype), window_strides=(1,),
                                   padding='VALID', dimension_numbers=('NWC', 'WIO', 'NWC'),
                                   feature_group_count=u.shape[-1])
    return out + b.astype(u.dtype), ext[:, ext.shape[1] - (k - 1):]

def ssd_scan(xh, dt, A, Bm, Cm, h0):
    b, L, H, P = xh.shape
    G, N = Bm.shape[2], Bm.shape[3]
    R = H // G
    q = min(CHUNK, L)
    nc = L // q
    f32 = jnp.float32
    xdt = (xh.astype(f32) * dt[..., None]).reshape(b, nc, q, G, R, P)
    acum = jnp.cumsum((dt * A).reshape(b, nc, q, G, R), axis=2)
    Bc = Bm.astype(f32).reshape(b, nc, q, G, N)
    Cc = Cm.astype(f32).reshape(b, nc, q, G, N)
    causal = jnp.tril(jnp.ones((q, q), dtype=bool))

    def step(h, inp):
        xdt_c, B_c, C_c, acum_c = inp
        ac = jnp.moveaxis(acum_c, 1, -1)
        seg = ac[..., :, None] - ac[..., None, :]
        decay = jnp.exp(jnp.where(causal, seg, -jnp.inf))
        cb = jnp.einsum('bign,bjgn->bgij', C_c, B_c)
        y_in = jnp.einsum('bgij,bgrij,bjgrp->bigrp', cb, decay, xdt_c)
        y_st = jnp.einsum('bign,bigr,bgrpn->bigrp', C_c, jnp.exp(acum_c), h)
        tail = jnp.exp(acum_c[:, -1:] - acum_c)
        h_new = (jnp.exp(acum_c[:, -1])[..., None, None] * h
                 + jnp.einsum('bjgn,bjgr,bjgrp->bgrpn', B_c, tail, xdt_c))
        return h_new, y_in + y_st

    h = h0.astype(f32).reshape(b, G, R, P, N)
    inputs = (jnp.moveaxis(xdt, 1, 0), jnp.moveaxis(Bc, 1, 0), jnp.moveaxis(Cc, 1, 0), jnp.moveaxis(acum, 1, 0))
    h_fin, ys = lax.scan(step, h, inputs)
    y = jnp.moveaxis(ys, 0, 1).reshape(b, L, H, P)
    return y, h_fin.reshape(b, H, P, N)

def conformer_conv_branch(glu_in, conv_buf, w_dw, b_dw, ln_g, ln_b, w_pw):
    u = glu_in[..., :D_CONV] * jax.nn.sigmoid(glu_in[..., D_CONV:])
    v, new_buf = causal_depthwise_conv(u, conv_buf, w_dw, b_dw)
    v = jax.nn.silu(layer_norm(v, ln_g, ln_b))
    return v @ w_pw, new_buf

def mamba2_branch(z, xbc, dt_raw, conv_buf, ssm_state, w_conv, b_conv, dt_bias, a_log, d_skip, norm_g, w_out):
    f32 = jnp.float32
    xbc_c, new_buf = causal_depthwise_conv(xbc, conv_buf, w_conv, b_conv)
    xbc_c = jax.nn.silu(xbc_c)
    xs, Bm, Cm = jnp.split(xbc_c, [D_INNER, D_INNER + N_GROUPS * D_STATE], axis=-1)
    b, L, _ = xs.shape
    xh = xs.reshape(b, L, N_SSM_HEADS, SSM_HEAD_DIM)
    Bm = Bm.reshape(b, L, N_GROUPS, D_STATE)
    Cm = Cm.reshape(b, L, N_GROUPS, D_STATE)
    dt = jax.nn.softplus(dt_raw.astype(f32) + dt_bias.astype(f32))
    A = -jnp.exp(a_log.astype(f32))
    y, h_fin = ssd_scan(xh, dt, A, Bm, Cm, ssm_state)
    y = (y + d_skip.astype(f32)[:, None] * xh.astype(f32)).reshape(b, L, D_INNER)
    g = (y * jax.nn.silu(z.astype(f32))).reshape(b, L, N_GROUPS, D_INNER // N_GROUPS)
    g = g * lax.rsqrt(jnp.mean(g * g, axis=-1, keepdims=True) + RMS_EPS)
    g = g.reshape(b, L, D_INNER) * norm_g.astype(f32)
    return g.astype(z.dtype) @ w_out, new_buf, h_fin.astype(z.dtype)

def encoder_forward(x, st_a, st_b, st_h, p):
    new_a, new_b, new_h = [], [], []
    for l in range(DEPTH):
        x = x + FFN_RES_WEIGHT * swiglu_ffn(rms_norm(x, p['norm_ffn1'][l]), p['ffn1_w_gate'][l],
                                            p['ffn1_w_up'][l], p['ffn1_w_down'][l])
        h = rms_norm(x, p['norm_mix'][l])
        proj = h @ p['w_in'][l]
        glu_in, z, xbc, dt_raw, gate_logits = jnp.split(proj, list(SPLIT_IDX), axis=-1)
        y_a, buf_a = conformer_conv_branch(glu_in, st_a[l], p['conv_a_w'][l], p['conv_a_b'][l],
                                           p['ln_conv_g'][l], p['ln_conv_b'][l], p['w_conv_a_out'][l])
        y_b, buf_b, h_fin = mamba2_branch(z, xbc, dt_raw, st_b[l], st_h[l], p['conv_b_w'][l], p['conv_b_b'][l],
                                          p['dt_bias'][l], p['a_log'][l], p['d_skip'][l],
                                          p['ssm_norm_g'][l], p['w_ssm_out'][l])
        gates = jax.nn.sigmoid(gate_logits.astype(jnp.float32))
        g_a, g_b = gates[..., :D_MODEL], gates[..., D_MODEL:]
        merged = (g_a * y_a.astype(jnp.float32) + g_b * y_b.astype(jnp.float32)).astype(x.dtype)
        x = x + merged @ p['w_out'][l]
        x = x + FFN_RES_WEIGHT * swiglu_ffn(rms_norm(x, p['norm_ffn2'][l]), p['ffn2_w_gate'][l],
                                            p['ffn2_w_up'][l], p['ffn2_w_down'][l])
        new_a.append(buf_a)
        new_b.append(buf_b)
        new_h.append(h_fin)
    y = rms_norm(x, p['norm_final'])
    return y, jnp.stack(new_a), jnp.stack(new_b), jnp.stack(new_h)

def setup_inputs(seed: int = 0) -> dict:
    key = jax.random.key(seed)
    ks = jax.random.split(key, 32)
    f32 = jnp.float32

    def nrm(k, shape, scale):
        return jax.random.normal(k, shape, f32) * scale

    def gain(k, shape):
        return 1.0 + 0.05 * jax.random.normal(k, shape, f32)

    dt0 = jnp.exp(jax.random.uniform(ks[20], (DEPTH, N_SSM_HEADS), f32)
                  * (math.log(0.1) - math.log(0.001)) + math.log(0.001))
    dt_bias = dt0 + jnp.log(-jnp.expm1(-dt0))
    return {
        "x_prompt": jax.random.normal(ks[0], (BATCH, SEQ, D_MODEL), f32),
        "x_sample": jax.random.normal(ks[1], (DEC_BATCH, DEC_SEQ, D_MODEL), f32),
        "state_conv_a": nrm(ks[2], (DEPTH, DEC_BATCH, CONV_A_WIDTH - 1, D_CONV), 0.5),
        "state_conv_b": nrm(ks[3], (DEPTH, DEC_BATCH, CONV_B_WIDTH - 1, D_XBC), 1.0),
        "state_ssm": nrm(ks[4], (DEPTH, DEC_BATCH, N_SSM_HEADS, SSM_HEAD_DIM, D_STATE), 0.5),
        "norm_ffn1": gain(ks[5], (DEPTH, D_MODEL)),
        "ffn1_w_gate": nrm(ks[6], (DEPTH, D_MODEL, D_FF), D_MODEL ** -0.5),
        "ffn1_w_up": nrm(ks[7], (DEPTH, D_MODEL, D_FF), D_MODEL ** -0.5),
        "ffn1_w_down": nrm(ks[8], (DEPTH, D_FF, D_MODEL), D_FF ** -0.5),
        "norm_mix": gain(ks[9], (DEPTH, D_MODEL)),
        "w_in": nrm(ks[10], (DEPTH, D_MODEL, D_IN_PROJ), D_MODEL ** -0.5),
        "conv_a_w": nrm(ks[11], (DEPTH, CONV_A_WIDTH, D_CONV), CONV_A_WIDTH ** -0.5),
        "conv_a_b": nrm(ks[12], (DEPTH, D_CONV), 0.01),
        "ln_conv_g": gain(ks[13], (DEPTH, D_CONV)),
        "ln_conv_b": nrm(ks[14], (DEPTH, D_CONV), 0.01),
        "w_conv_a_out": nrm(ks[15], (DEPTH, D_CONV, D_MODEL), D_CONV ** -0.5),
        "conv_b_w": nrm(ks[16], (DEPTH, CONV_B_WIDTH, D_XBC), CONV_B_WIDTH ** -0.5),
        "conv_b_b": nrm(ks[17], (DEPTH, D_XBC), 0.01),
        "dt_bias": dt_bias,
        "a_log": jnp.log(jax.random.uniform(ks[18], (DEPTH, N_SSM_HEADS), f32, 1.0, 16.0)),
        "d_skip": gain(ks[19], (DEPTH, N_SSM_HEADS)),
        "ssm_norm_g": gain(ks[21], (DEPTH, D_INNER)),
        "w_ssm_out": nrm(ks[22], (DEPTH, D_INNER, D_MODEL), D_INNER ** -0.5),
        "w_out": nrm(ks[23], (DEPTH, D_MODEL, D_MODEL), D_MODEL ** -0.5),
        "norm_ffn2": gain(ks[24], (DEPTH, D_MODEL)),
        "ffn2_w_gate": nrm(ks[25], (DEPTH, D_MODEL, D_FF), D_MODEL ** -0.5),
        "ffn2_w_up": nrm(ks[26], (DEPTH, D_MODEL, D_FF), D_MODEL ** -0.5),
        "ffn2_w_down": nrm(ks[27], (DEPTH, D_FF, D_MODEL), D_FF ** -0.5),
        "norm_final": gain(ks[28], (D_MODEL,)),
    }

def reference(x_prompt, x_sample, state_conv_a, state_conv_b, state_ssm,
              norm_ffn1, ffn1_w_gate, ffn1_w_up, ffn1_w_down, norm_mix, w_in,
              conv_a_w, conv_a_b, ln_conv_g, ln_conv_b, w_conv_a_out,
              conv_b_w, conv_b_b, dt_bias, a_log, d_skip, ssm_norm_g, w_ssm_out,
              w_out, norm_ffn2, ffn2_w_gate, ffn2_w_up, ffn2_w_down, norm_final):
    p = dict(norm_ffn1=norm_ffn1, ffn1_w_gate=ffn1_w_gate, ffn1_w_up=ffn1_w_up, ffn1_w_down=ffn1_w_down,
             norm_mix=norm_mix, w_in=w_in, conv_a_w=conv_a_w, conv_a_b=conv_a_b, ln_conv_g=ln_conv_g,
             ln_conv_b=ln_conv_b, w_conv_a_out=w_conv_a_out, conv_b_w=conv_b_w, conv_b_b=conv_b_b,
             dt_bias=dt_bias, a_log=a_log, d_skip=d_skip, ssm_norm_g=ssm_norm_g, w_ssm_out=w_ssm_out,
             w_out=w_out, norm_ffn2=norm_ffn2, ffn2_w_gate=ffn2_w_gate, ffn2_w_up=ffn2_w_up,
             ffn2_w_down=ffn2_w_down, norm_final=norm_final)
    bp = x_prompt.shape[0]
    dtp = x_prompt.dtype
    zero_a = jnp.zeros((DEPTH, bp, CONV_A_WIDTH - 1, D_CONV), dtp)
    zero_b = jnp.zeros((DEPTH, bp, CONV_B_WIDTH - 1, D_XBC), dtp)
    zero_h = jnp.zeros((DEPTH, bp, N_SSM_HEADS, SSM_HEAD_DIM, D_STATE), dtp)
    y_prompt, new_conv_a_prompt, new_conv_b_prompt, new_ssm_prompt = encoder_forward(
        x_prompt, zero_a, zero_b, zero_h, p)
    y_sample, new_conv_a_sample, new_conv_b_sample, new_ssm_sample = encoder_forward(
        x_sample, state_conv_a, state_conv_b, state_ssm, p)
    return (y_prompt, y_sample, new_conv_a_prompt, new_conv_b_prompt, new_ssm_prompt,
            new_conv_a_sample, new_conv_b_sample, new_ssm_sample)


_drawn_inputs = setup_inputs


def setup_inputs(seed=0):
    import zlib

    import numpy as np

    out = dict(_drawn_inputs(seed))
    spreads = {}
    factors = {'conv_a_b': 8.0,
     'ln_conv_g': 3.281,
     'ln_conv_b': 8.0,
     'conv_b_b': 3.439,
     'd_skip': 8.768,
     'norm_ffn2': 3.316}
    for name, (base, spread) in spreads.items():
        noise = np.random.default_rng([zlib.crc32(name.encode()), seed]).standard_normal(out[name].shape)
        drawn = base * np.exp(spread * noise) if base else spread * noise
        out[name] = __import__('jax').numpy.asarray(drawn.astype(out[name].dtype))
    for name, factor in factors.items():
        out[name] = (out[name] * factor).astype(out[name].dtype)
    return out
```

```python
from contextlib import ExitStack

import concourse.bass as bass
from concourse import mybir

F32 = mybir.dt.float32
F32R = mybir.dt.float32r
ALU = mybir.AluOpType
ACT = mybir.ActivationFunctionType

P = 128
TP, NB, TS = 512, 8, 16
T = TP + NB * TS
TH = T // 2
NT = T // P
LAST = NT - 1
DM = 1024
KM = DM // P
PARTS = (8, 8, 6)
NFF = sum(PARTS)
DFF = NFF * P
KA, KB = 31, 4
HA, HB = KA - 1, KB - 1
G, HG, PD, NS = 4, 8, 64, 128
H = G * HG
GC = HG * PD // P
NX = GC + 2
EA, EB = HA + TP, HB + TP
WA, WB = EA + NB * (HA + TS), EB + NB * (HB + TS)
RMS_EPS, LN_EPS = 1e-6, 1e-5

J_U0, J_Z, J_U1, J_O = NX, NX + 2, NX + 2 + GC, NX + 4 + GC
GJ = J_O + KM
TAPS = {0: dict(zip(range(8, 14), (4, 4, 4, 4, 5, 10))), 1: dict(zip(range(14, 22), (4, 4, 4, 4, 4, 4, 4, 3)))}

FFN_HALVES = sum(n + KM // 2 for n in PARTS)
MIX_HALF = FFN_HALVES
GATE_HALF = MIX_HALF + G * GJ // 2
FFN2_HALF = GATE_HALF + 4 * KM // 2

P_CB, P_CA = 0, NX * (KB + 1)
P_D = P_CA + 2 * (KA + 1)
P_N = P_D + GC
NPAR = P_N + GC
TRI, TRI_S, ONES, BLK_S, IDENT = range(5)
N_FFN1, N_MIX, N_GROUP, N_MEAN, N_LN, N_FFN2, N_OUT = 0, 1, 2, 6, 7, 8, 9
Q_FFN1, Q_MIX, Q_GROUP, Q_LN, Q_FFN2, Q_OUT = 0, KM, 2 * KM, 2 * KM + G * GC, 3 * KM + G * GC, 4 * KM + G * GC
S_FFN1, S_MIX, S_LN, S_FFN2 = 0, KM, 2 * KM, 3 * KM


def build(nc, d):
    with ExitStack() as ctx:
        def sb(name, shape, dt=F32, stack=ctx):
            return stack.enter_context(nc.sbuf_tensor(name, shape, dt))

        def sem(name):
            return ctx.enter_context(nc.semaphore(name))

        xa_hi = sb("xa_hi", [P, KM, T], F32R)
        xa_lo = sb("xa_lo", [P, KM, T], F32R)
        w_raw = sb("w_raw", [P, 2, KM * P])
        w_hi = sb("w_hi", [P, 2, KM * P], F32R)
        w_lo = sb("w_lo", [P, 2, KM * P], F32R)
        const = sb("const", [P, 5, P])
        bmask = sb("bmask", [P, NB])
        gains = sb("gains", [P, 6, KM])
        acc = sb("acc", [P, T])
        sq = sb("sq", [P, 2, T])
        pair = sb("pair", [P, 2, T])
        var, rsq0 = pair[:, 0], pair[:, 1]
        conv_b = pair
        rstd = sb("rstd", [P, T])
        par = sb("par", [P, G, NPAR])
        parg = sb("parg", [P, NPAR])
        halo_b = sb("halo_b", [P, G, NX, NB * HB])
        new_b = sb("new_b", [P, G, NX, HB + NB * HB])
        tok = sb("tok", [P, 3, NT, H])
        tokg = sb("tokg", [P, 3, NT, HG])
        dt_par = sb("dt_par", [P, 3, H])

        def here(*tensors):
            with ExitStack() as stack:
                return [sb(*t, stack=stack) for t in tensors]

        h_hi, h_lo = here(("h_hi", [P, KM, T], F32R), ("h_lo", [P, KM, T], F32R))
        merged_hi, = here(("merged_hi", [P, KM, T], F32R))
        v = sb("v", [P, KM, T])
        yb = sb("yb", [P, KM, T])
        x, gate_s, silu_g, up_s, hid = here(
            ("x", [P, KM, T]), ("gate_s", [P, T]), ("silu_g", [P, T]), ("up_s", [P, T]), ("hid", [P, T]))
        _, gate_a, gate_b, prod = here(
            ("x_place", [P, KM, T]), ("gate_a", [P, KM, T]), ("gate_b", [P, 2, T]), ("prod", [P, T]))
        _, merged_lo = here(("x_place2", [P, KM, T]), ("merged_lo", [P, KM, T], F32R))
        ext_b = sb("ext_b", [P, 2, WB])
        ext_a = sb("ext_a", [P, WA])
        sig = sb("sig", [P, T])
        h_pr = sb("h_pr", [P, HG * PD])
        bc = sb("bc", [P, 2, T])
        gn_hi, = here(("gn_hi", [P, GC, T], F32R))
        xs = sb("xs", [P, GC, T])
        gn_lo, = here(("gn_lo", [P, GC, T], F32R))
        acb = sb("acb", [P, 2, HG, P])
        mdec = sb("mdec", [P, HG, P])
        z = sb("z", [P, GC, T])
        cum_sb, wdt_raw, wdt_hi, wdt_lo = here(
            ("cum_sb", [P, T]), ("wdt_raw", [P, KM * H]), ("wdt_hi", [P, KM * H], F32R), ("wdt_lo", [P, KM * H], F32R))
        y = sb("y", [P, GC, T])
        dts, = here(("dts", [P, 6, NT * H]))
        xdt = sb("xdt", [P, HG * PD])
        xtl = sb("xtl", [P, HG * PD])
        btok = sb("btok", [P, NS])
        cbm = sb("cbm", [P, P])
        ach = sb("ach", [P, 2, GC, P])
        el = sb("el", [P, 2, HG, NB])
        h_smp = sb("h_smp", [P, 2, HG * PD])
        x_spill = nc.dram_tensor("x_spill", (KM, P, T), F32).ap()
        cum_dram = nc.dram_tensor("cum_dram", (G, GC, 2, T), F32).ap()
        psj = ctx.enter_context(nc.psum_tensor("psj", [P, 2, 2, 512], F32))
        pab = ctx.enter_context(nc.psum_tensor("pab", [P, 2, 512], F32))
        pc = ctx.enter_context(nc.psum_tensor("pc", [P, 512], F32))
        pd = ctx.enter_context(nc.psum_tensor("pd", [P, 512], F32))
        pa, pb = pab[:, 0], pab[:, 1]

        def job_out(b):
            return psj[:, b, :, 0:TH]

        def halved(ap):
            return ap.rearrange("p (u t) -> p u t", u=2)

        def seqs(ap):
            return ap.rearrange("p (b t) -> p b t", b=NB)

        raw_in = [sem("raw_in0"), sem("raw_in1")]
        hi_done = sem("hi_done")
        lo_done = sem("lo_done")
        job_done = sem("job_done")
        evac_done = [sem("evac0"), sem("evac1")]
        const_in, par_in, x_in = sem("const_in"), sem("par_in"), sem("x_in")
        silu_ready = sem("silu_ready")
        hid_ready, hhi_ready, hlo_ready = sem("hid_ready"), sem("hhi_ready"), sem("hlo_ready")
        sq_ready, acc_ready = sem("sq_ready"), sem("acc_ready")
        nin_ready = sem("nin_ready")
        vs_ready = sem("vs_ready")
        xhi_ready, xlo_ready = sem("xhi_ready"), sem("xlo_ready")
        sum_ready, var_ready, rsq_ready, rstd_ready = sem("sum_ready"), sem("var_ready"), sem("rsq_ready"), sem("rstd_ready")
        ln_step, newton_step = sem("ln_step"), sem("newton_step")
        spilled, x_back = sem("spilled"), sem("x_back")
        wdt_in, wdt_split, wdt_lo_ready, dt_mm = sem("wdt_in"), sem("wdt_split"), sem("wdt_lo_ready"), sem("dt_mm")
        dt_act, dt_dve, cum_mm = sem("dt_act"), sem("dt_dve"), sem("cum_mm")
        cum_copied, cum_out, tok_done = sem("cum_copied"), sem("cum_out"), sem("tok_done")
        cleared = sem("cleared")
        parg_ready, tokg_ready = sem("parg_ready"), sem("tokg_ready")
        extb_ready = sem("extb_ready")
        tap_b = sem("tap_b")
        convb_ready = sem("convb_ready")
        xbc_ready = sem("xbc_ready")
        halo_a_in = sem("halo_a_in")
        u_part = sem("u_part")
        u_saved = sem("u_saved")
        tap_a = sem("tap_a")
        conva_ready = sem("conva_ready")
        tile_in = [sem(f"tile_in{t}") for t in range(NT)]
        turned = sem("turned")
        btok_ready, xdt_ready, cbm_ready, m_ready = sem("btok_ready"), sem("xdt_ready"), sem("cbm_ready"), sem("m_ready")
        dec_step, dec_ready = sem("dec_step"), sem("dec_ready")
        y_mm = sem("y_mm")
        s_mm = sem("s_mm")
        state_step, state_ready = sem("state_step"), sem("state_ready")
        y_step = sem("y_step")
        y_done = sem("y_done")
        bm_ready = sem("bm_ready")
        hs_in = [sem("hs_in0"), sem("hs_in1")]
        hs_mm, hs_step = sem("hs_mm"), sem("hs_step")
        hs_new = sem("hs_new")
        hs_out = [sem("hs_out0"), sem("hs_out1")]
        hp_out = sem("hp_out")
        stored = sem("stored")
        gz_ready = sem("gz_ready")
        gnhi_ready, gnlo_ready = sem("gnhi_ready"), sem("gnlo_ready")
        yo_step = sem("yo_step")
        yb_ready = sem("yb_ready")
        gb_ready, gb_used = sem("gb_ready"), sem("gb_used")
        vsum_step, vc_ready = sem("vsum_step"), sem("vc_ready")
        prod_step, merge_ready, mhi_ready, mlo_ready = sem("prod_step"), sem("merge_ready"), sem("mhi_ready"), sem("mlo_ready")
        out_ready, saved = sem("out_ready"), sem("saved")
        pool_passed = sem("pool_passed")

        def x_updated(eng, end_half, c):
            eng.wait_ge(evac_done[c % 2], end_half - KM // 2 + c // 2 + 2)

        block = ctx.enter_context(nc.Block())

        @block.sync
        def _(sp):
            def load(half, b, src, width=KM * P):
                sp.wait_ge(lo_done, 2 * half + b + 1)
                sp.dma_start(w_raw[:, b, 0:width], src).then_inc(raw_in[b], 16)

            sp.dma_start(gains[:], d["gains"]).then_inc(const_in, 16)
            for c in range(KM):
                sp.dma_start(x[:, c, :], d["x"][c]).then_inc(x_in, 16)
            half = 0
            for f in range(2):
                chunk = 0
                for p, n in enumerate(PARTS):
                    with sp.Fori(0, n) as i:
                        for b in range(2):
                            load(half + i, b, d["w_gu"][f, i + chunk, b])
                    half += n
                    chunk += n
                    w_down = d["w_down"][f, p] if n == KM else d["w_down_last"][f]
                    with sp.Fori(0, KM // 2) as j:
                        for b in range(2):
                            load(half + j, b, w_down[j, b], n * P)
                    half += KM // 2
                if f == 0:
                    with sp.Fori(0, G) as g:
                        for k in range(GJ):
                            src = d["w_mix"][g, k] if k < J_O else d["w_ssm"][g, k - J_O]
                            load(MIX_HALF + g * (GJ // 2) + k // 2, k % 2, src, KM * P if k < J_O else GC * P)
                    with sp.Fori(0, 2 * KM) as i:
                        for b in range(2):
                            load(GATE_HALF + i, b, d["w_tail"][i, b])
                    half = FFN2_HALF

        @block.gpsimd
        def _(pool):
            pool.sem_inc(stored, 1)
            pool.dma_start(const[:], d["const"]).then_inc(par_in, 16)
            pool.dma_start(par[:], d["par"]).then_inc(par_in, 16)
            pool.dma_start(halo_b[:], d["halo_b"]).then_inc(par_in, 16)
            pool.dma_start(bmask[:], d["bmask"]).then_inc(par_in, 16)
            pool.dma_start(wdt_raw[:], d["w_dt"]).then_inc(wdt_in, 16)
            pool.dma_start(dt_par[:, 0], d["dt_bias"].partition_broadcast(P)).then_inc(wdt_in, 16)
            pool.dma_start(dt_par[:, 1], d["a_log"].partition_broadcast(P)).then_inc(wdt_in, 16)
            for c in range(KM):
                x_updated(pool, MIX_HALF, c)
                pool.dma_start(x_spill[c], x[:, c, :]).then_inc(spilled, 16)
            pool.wait_ge(cum_copied, 3)
            pool.dma_start(cum_dram.rearrange("g c e t -> (g c e) t"), cum_sb[0:H, :]).then_inc(cum_out, 16)
            pool.wait_ge(cum_out, 16)
            pool.wait_ge(cleared, 3)

            def group(g):
                def wait(semaphore, value):
                    pool.wait_ge(semaphore, value)
                    pool.sem_inc(pool_passed, 1)

                def sample_in(b):
                    if b >= 2:
                        wait(hs_out[b % 2], 16 * (NB // 2) * g + 16 * (b // 2))
                    pool.dma_start(h_smp[:, b % 2], d["h_sample"][g, b]).then_inc(hs_in[b % 2], 16)

                def tile(t):
                    cols = slice(t * P, (t + 1) * P)
                    if t >= 2:
                        wait(y_done, NT * g + t)
                    pool.dma_start(acb[:, t % 2], cum_dram[g].rearrange("c e t -> (c e) t")[:, cols]
                                   .partition_broadcast(P)).then_inc(tile_in[t], 16)
                    for e in range(2):
                        pool.dma_start(ach[e * PD:(e + 1) * PD, t % 2], cum_dram[g, :, e, cols]
                                       .partition_broadcast(PD)).then_inc(tile_in[t], 16)

                def halo_a(c):
                    wait(conva_ready, 2 * g + c + 1)
                    if c == 1:
                        wait(u_saved, 32 * (2 * g + 1))
                    pool.dma_start(seqs(ext_a[:, EA:])[:, :, 0:HA], d["halo_a"][2 * g + c]).then_inc(halo_a_in, 16)

                def save_a(c):
                    wait(halo_a_in, 16 * (2 * g + c + 1))
                    wait(u_part, 2 * (2 * g + c + 1))
                    wait(evac_done[1], MIX_HALF + g * (GJ // 2) + (J_U0, J_U1)[c] // 2 + 2)
                    pool.dma_start(d["new_a_prompt"][2 * g + c], ext_a[:, TP:EA]).then_inc(u_saved, 16)
                    pool.dma_start(d["new_a_sample"][2 * g + c], seqs(ext_a[:, EA:])[:, :, TS:]).then_inc(u_saved, 16)

                halo_a(0)
                wait(job_done, 2 * MIX_HALF + g * GJ + 2)
                tile(0)
                tile(1)
                sample_in(0)
                sample_in(1)
                save_a(0)
                for t in range(2, NT):
                    tile(t)
                wait(state_ready, LAST * g + LAST)
                pool.dma_start(d["new_h_prompt"][g], h_pr[:]).then_inc(hp_out, 16)
                for b in range(NB):
                    wait(hs_new, NB * g + b + 3)
                    pool.dma_start(d["new_h_sample"][g, b], h_smp[:, b % 2]).then_inc(hs_out[b % 2], 16)
                    if b + 2 < NB:
                        sample_in(b + 2)
                halo_a(1)
                save_a(1)
                for s in range(2):
                    wait(hs_out[s], 16 * (NB // 2) * (g + 1))
                wait(hp_out, 16 * (g + 1))
                wait(u_saved, 64 * (g + 1))
                pool.sem_inc(stored, 1)

            with pool.Fori(0, G) as g:
                group(g)
            pool.wait_ge(conva_ready, 2 * G + 1)
            pool.wait_ge(yb_ready, KM * G)
            for c in range(KM):
                pool.dma_start(x[:, c, :], x_spill[c]).then_inc(x_back, 16)
            pool.dma_start(d["new_b"], new_b[:]).then_inc(saved, 16)
            for c in range(KM):
                pool.wait_ge(out_ready, c + 1)
                pool.dma_start(d["y"][c], x[:, c, :]).then_inc(saved, 16)
            pool.wait_ge(saved, 16 * (KM + 1))

        @block.scalar
        def _(act):
            def split_hi(half, b, width=KM * P):
                act.wait_ge(raw_in[b], 16 * half + 16)
                act.wait_ge(job_done, 2 * half + b + 1)
                nc.scalar.copy(w_hi[:, b, 0:width], w_raw[:, b, 0:width]).then_inc(hi_done, 1)

            def job_ended(half, b):
                act.wait_ge(job_done, 2 * half + b + 3)

            def square(m, s, src):
                if not isinstance(m, int) or m >= 2:
                    act.wait_ge(acc_ready, m - 1)
                nc.scalar.activation(sq[:, s], src, ACT.Square).then_inc(sq_ready, 1)

            def inverse_root(e, i):
                act.wait_ge(var_ready, i + 1)
                nc.scalar.activation(rsq0, var, ACT.Ln).then_inc(ln_step, 1)
                act.wait_ge(ln_step, i + 1)
                nc.scalar.activation(rsq0, rsq0, ACT.Exp, scale=-0.5).then_inc(rsq_ready, 1)

            def xa_high(m, src, gain, c):
                nc.scalar.activation(xa_hi[:, c, :], src, ACT.Copy,
                                     scale=gains[:, gain, c:c + 1]).then_inc(xhi_ready, 1)

            def ffn(f, norm, updated):
                half, q0 = f * FFN2_HALF, NFF * f
                for p, n in enumerate(PARTS):
                    def gate_up(i, next_width=KM * P, first=False):
                        split_hi(half + i, 1)
                        if first:
                            norm()
                        act.wait_ge(evac_done[0], half + i + 2)
                        nc.scalar.activation(silu_g[:], gate_s[:], ACT.Silu).then_inc(silu_ready, 1)
                        split_hi(half + i + 1, 0, next_width)
                        act.wait_ge(hid_ready, i + (q0 + 1))
                        nc.scalar.copy(h_hi[:, i, :], hid[:]).then_inc(hhi_ready, 1)

                    if p == 0:
                        gate_up(0, first=True)
                    with act.Fori(1 if p == 0 else 0, n - 1) as i:
                        gate_up(i)
                    gate_up(n - 1, n * P)
                    half += n
                    q0 += n

                    def down(j, next_width):
                        split_hi(half + j, 1, n * P)
                        if n < KM:
                            updated(2 * j)
                        if next_width:
                            split_hi(half + j + 1, 0, next_width)
                        if n < KM:
                            updated(2 * j + 1)

                    if n == KM:
                        with act.Fori(0, KM // 2 - 1) as j:
                            down(j, n * P)
                        down(KM // 2 - 1, KM * P)
                    else:
                        for j in range(KM // 2):
                            down(j, n * P if j < KM // 2 - 1 else (0 if f else KM * P))
                    half += KM // 2

            act.sem_inc(xbc_ready, 2)
            act.wait_ge(const_in, 16)
            split_hi(0, 0)
            for c in range(KM):
                act.wait_ge(x_in, 16 * KM)
                square(c, c % 2, x[:, c, :])
                xa_high(S_FFN1 + c, x[:, c, :], 0, c)

            def squares_for_mix(c):
                x_updated(act, MIX_HALF, c)
                square(Q_MIX + c, c % 2, x[:, c, :])

            ffn(0, lambda: inverse_root(N_FFN1, 0), squares_for_mix)
            inverse_root(N_MIX, 1)
            for c in range(KM):
                act.wait_ge(nin_ready, c + 1)
                xa_high(S_MIX + c, sq[:, c % 2], 1, c)
            act.wait_ge(wdt_in, 48)
            nc.scalar.copy(wdt_hi[:], wdt_raw[:]).then_inc(wdt_split, 1)
            act.wait_ge(dt_dve, 1)
            nc.scalar.activation(dts[:, 1], dts[:, 0], ACT.Abs).then_inc(dt_act, 1)
            act.wait_ge(dt_act, 1)
            nc.scalar.activation(dts[:, 1], dts[:, 1], ACT.Exp, scale=-1.0).then_inc(dt_act, 1)
            nc.scalar.activation(dt_par[:, 2], dt_par[:, 1], ACT.Exp).then_inc(dt_act, 1)
            act.wait_ge(dt_dve, 2)
            nc.scalar.activation(dts[:, 3], dts[:, 2], ACT.Ln).then_inc(dt_act, 1)
            act.wait_ge(cum_mm, 1)
            nc.scalar.copy(cum_sb[0:H, 0:TP], pb[0:H, :]).then_inc(cum_copied, 1)
            nc.scalar.copy(cum_sb[0:H, TP:T], pc[0:H, 0:P]).then_inc(cum_copied, 1)
            nc.scalar.copy(tok[:, 1], pa[:, 0:NT * H].rearrange("p (t h) -> p t h", t=NT)).then_inc(cum_copied, 1)
            act.wait_ge(tok_done, 1)
            nc.scalar.activation(tok[:, 2], tok[:, 2], ACT.Exp).then_inc(tok_done, 1)
            act.wait_ge(tok_done, 3)
            act.wait_ge(spilled, 16 * KM)

            def group(g):
                def at(k):
                    return MIX_HALF + g * (GJ // 2) + k // 2, k % 2

                def next_hi(k):
                    split_hi(*at(k + 1), KM * P if k + 1 < J_O or k + 1 == GJ else GC * P)

                def xbc_in(k):
                    s = k % 2
                    job_ended(*at(k))
                    act.wait_ge(convb_ready, NX * g + k + 1)
                    smp, ps_smp = seqs(ext_b[:, s, EB:]), seqs(psj[:, s, 1, TP - TH:TH])
                    nc.scalar.copy(ext_b[:, s, HB:HB + TH], psj[:, s, 0, 0:TH]).then_inc(extb_ready, 1)
                    nc.scalar.copy(ext_b[:, s, HB + TH:EB], psj[:, s, 1, 0:TP - TH]).then_inc(extb_ready, 1)
                    nc.scalar.copy(smp[:, :, 0:HB], seqs(halo_b[:, g, k])).then_inc(extb_ready, 1)
                    nc.scalar.copy(new_b[:, g, k, 0:HB], psj[:, s, 1, TP - TH - HB:TP - TH]).then_inc(extb_ready, 1)
                    nc.scalar.copy(seqs(new_b[:, g, k, HB:]), ps_smp[:, :, TS - HB:]).then_inc(extb_ready, 1)
                    nc.scalar.copy(smp[:, :, HB:], ps_smp).then_inc(evac_done[s], 1)

                def xbc_silu(k):
                    act.wait_ge(tap_b, (2 * KB - 1) * (NX * g + k + 1))
                    act.wait_ge(convb_ready, NX * g + k + 3)
                    dst = xs[:, k, :] if k < GC else bc[:, k - GC, :]
                    nc.scalar.activation(dst, conv_b[:, k % 2], ACT.Silu).then_inc(xbc_ready, 1)

                def glu_gate(k):
                    job_ended(*at(k))
                    nc.scalar.activation(halved(sig[:]), job_out(k % 2), ACT.Sigmoid).then_inc(evac_done[k % 2], 1)

                def decay(t):
                    s, n = t % 2, NT * g + t
                    act.wait_ge(tile_in[t], 48 * g + 48)
                    if t < 2:
                        act.wait_ge(hs_new, NB * g + 2)
                    else:
                        act.wait_ge(state_ready, LAST * g + t - 1)
                    ends = slice(P - 1, P) if t < LAST else slice(TS - 1, P, TS)
                    width = 1 if t < LAST else NB
                    nc.scalar.activation(el[:, s, :, 0:width], acb[:, s, :, ends], ACT.Exp).then_inc(dec_step, 1)
                    act.wait_ge(dec_step, (HG + 1) * n + 1)
                    for j in range(HG):
                        nc.scalar.activation(acb[:, s, j], acb[:, s, j], ACT.Relu, scale=-1.0,
                                             bias=tokg[:, 1, t, j:j + 1]).then_inc(dec_step, 1)
                    nc.scalar.activation(ach[:, s], ach[:, s], ACT.Exp).then_inc(dec_ready, 1)
                    act.wait_ge(dec_step, (HG + 1) * (n + 1))
                    nc.scalar.activation(acb[:, s], acb[:, s], ACT.Exp, scale=-1.0).then_inc(dec_ready, 1)

                def btok_out(t):
                    act.wait_ge(turned, NT * g + t + 1)
                    act.wait_ge(s_mm, LAST * g + t + 1)
                    act.wait_ge(cbm_ready, NT * g + t + 1)
                    nc.scalar.copy(btok[:], pb[:, 0:NS]).then_inc(btok_ready, 1)

                act.wait_ge(conva_ready, 2 * g + 1)
                nc.scalar.copy(parg[:], par[:, g]).then_inc(parg_ready, 1)
                nc.scalar.copy(tokg[:].rearrange("p a t h -> p (a t) h"),
                               tok[:].rearrange("p a t h -> p (a t) h")[:, :, bass.ds(g * HG, HG)]
                               ).then_inc(tokg_ready, 1)
                act.wait_ge(tokg_ready, g + 1)
                for k in range(NX):
                    next_hi(k)
                    xbc_in(k)
                    if k >= 1:
                        xbc_silu(k - 1)
                next_hi(J_U0)
                xbc_silu(NX - 1)
                glu_gate(J_U0)
                next_hi(J_U0 + 1)
                decay(0)
                btok_out(0)
                for c in range(GC):
                    k = J_Z + c
                    next_hi(k)
                    decay(c + 1)
                    job_ended(*at(k))
                    nc.scalar.activation(halved(z[:, c]), job_out(k % 2), ACT.Silu).then_inc(evac_done[k % 2], 1)
                    btok_out(c + 1)
                next_hi(J_U1)
                glu_gate(J_U1)
                next_hi(J_U1 + 1)
                for c in range(GC):
                    act.wait_ge(gz_ready, GC * g + c + 1)
                    square(Q_GROUP + GC * g + c, c % 2, y[:, c])
                    nc.scalar.activation(gn_hi[:, c], y[:, c], ACT.Copy,
                                         scale=parg[:, P_N + c:P_N + c + 1]).then_inc(gnhi_ready, 1)
                next_hi(J_O)
                inverse_root(N_GROUP + g, 2 + g)
                for k in range(J_O + 1, GJ):
                    next_hi(k)

            with act.Fori(0, G) as g:
                group(g)

            half = GATE_HALF

            act.wait_ge(yb_ready, KM * G)
            act.wait_ge(conva_ready, 2 * G + 1)
            for c in range(KM):
                split_hi(half + (c + 1) // 2, (c + 1) % 2)
                job_ended(half + c // 2, c % 2)
                nc.scalar.activation(halved(gate_a[:, c]), job_out(c % 2), ACT.Sigmoid).then_inc(evac_done[c % 2], 1)
                if c == 3:
                    for i in range(KM):
                        act.wait_ge(vc_ready, i + 1)
                        square(Q_LN + i, i % 2, v[:, i])
            inverse_root(N_LN, 6)
            half += KM // 2
            for c in range(KM):
                split_hi(half + (c + 1) // 2, (c + 1) % 2)
                job_ended(half + c // 2, c % 2)
                if c >= 2:
                    act.wait_ge(gb_used, c - 1)
                nc.scalar.activation(halved(gate_b[:, c % 2]), job_out(c % 2), ACT.Sigmoid).then_inc(evac_done[c % 2], 1)
                act.wait_ge(nin_ready, KM + c + 1)
                nc.scalar.activation(v[:, c], v[:, c], ACT.Silu, bias=gains[:, 5, c:c + 1],
                                     scale=gains[:, 4, c:c + 1]).then_inc(vs_ready, 1)
            half += KM // 2
            for c in range(KM):
                act.wait_ge(vs_ready, c + 1)
                nc.scalar.copy(xa_hi[:, c], v[:, c]).then_inc(xhi_ready, 1)
            for c in range(KM):
                split_hi(half + (c + 1) // 2, (c + 1) % 2)
                act.wait_ge(merge_ready, c + 1)
                nc.scalar.copy(merged_hi[:, c], yb[:, c]).then_inc(mhi_ready, 1)
            half += KM // 2
            for c in range(KM):
                split_hi(half + (c + 1) // 2, (c + 1) % 2)
                x_updated(act, FFN2_HALF, c)
                square(Q_FFN2 + c, c % 2, x[:, c])
                xa_high(S_FFN2 + c, x[:, c], 2, c)

            def squares_for_output(c):
                x_updated(act, FFN2_HALF + FFN_HALVES, c)
                square(Q_OUT + c, c % 2, x[:, c, :])

            ffn(1, lambda: inverse_root(N_FFN2, 7), squares_for_output)
            inverse_root(N_OUT, 8)

        @block.vector
        def _(dve):
            def split_lo(half, b, width=KM * P):
                dve.wait_ge(hi_done, 2 * half + b + 1)
                nc.vector.tensor_tensor(w_lo[:, b, 0:width], w_raw[:, b, 0:width],
                                        w_hi[:, b, 0:width].bitcast(F32), ALU.subtract).then_inc(lo_done, 1)

            def job_ended(half, b):
                dve.wait_ge(job_done, 2 * half + b + 3)

            def accumulate(m, s, first):
                dve.wait_ge(sq_ready, m + 1)
                if first:
                    nc.vector.tensor_copy(acc[:], sq[:, s]).then_inc(acc_ready, 1)
                else:
                    dve.wait_ge(acc_ready, m)
                    nc.vector.tensor_tensor(acc[:], acc[:], sq[:, s], ALU.add).then_inc(acc_ready, 1)

            def variance(e, width, eps):
                dve.wait_ge(sum_ready, e + 1)
                nc.vector.tensor_scalar(halved(var), pab[:, :, 0:TH], 1.0 / width, eps,
                                        ALU.mult, ALU.add).then_inc(var_ready, 1)

            def newton(i):
                dve.wait_ge(rsq_ready, i + 1)
                nc.vector.scalar_tensor_tensor(rstd[:], var, -0.5, rsq0, ALU.mult, ALU.mult).then_inc(newton_step, 1)
                dve.wait_ge(newton_step, 2 * i + 1)
                nc.vector.tensor_tensor(rstd[:], rstd[:], rsq0, ALU.mult).then_inc(newton_step, 1)
                dve.wait_ge(newton_step, 2 * i + 2)
                nc.vector.scalar_tensor_tensor(rstd[:], rstd[:], 1.5, rsq0, ALU.add, ALU.mult).then_inc(rstd_ready, 1)
                dve.wait_ge(rstd_ready, i + 1)

            def xa_low(m, src, gain, c):
                dve.wait_ge(xhi_ready, m + 1)
                nc.vector.scalar_tensor_tensor(xa_lo[:, c], src, gains[:, gain, c:c + 1], xa_hi[:, c].bitcast(F32),
                                               ALU.mult, ALU.subtract).then_inc(xlo_ready, 1)

            def ffn(f, norm, updated):
                half, q0 = f * FFN2_HALF, NFF * f
                for p, n in enumerate(PARTS):
                    def gate_up(i, next_width=KM * P, first=False):
                        split_lo(half + i, 1)
                        if first:
                            norm()
                        job_ended(half + i, 0)
                        nc.vector.tensor_tensor(halved(gate_s[:]), job_out(0), halved(rstd[:]),
                                                ALU.mult).then_inc(evac_done[0], 1)
                        split_lo(half + i + 1, 0, next_width)
                        job_ended(half + i, 1)
                        nc.vector.tensor_tensor(halved(up_s[:]), job_out(1), halved(rstd[:]),
                                                ALU.mult).then_inc(evac_done[1], 1)
                        dve.wait_ge(evac_done[1], half + i + 2)
                        dve.wait_ge(silu_ready, i + (q0 + 1))
                        nc.vector.tensor_tensor(hid[:], silu_g[:], up_s[:], ALU.mult).then_inc(hid_ready, 1)
                        dve.wait_ge(hhi_ready, i + (q0 + 1))
                        nc.vector.tensor_tensor(h_lo[:, i, :], hid[:], h_hi[:, i, :].bitcast(F32),
                                                ALU.subtract).then_inc(hlo_ready, 1)

                    if p == 0:
                        gate_up(0, first=True)
                    with dve.Fori(1 if p == 0 else 0, n - 1) as i:
                        gate_up(i)
                    gate_up(n - 1, n * P)
                    half += n
                    q0 += n

                    def down(j, next_width):
                        for b in range(2):
                            if b == 0:
                                split_lo(half + j, 1, n * P)
                            elif next_width:
                                split_lo(half + j + 1, 0, next_width)
                            job_ended(half + j, b)
                            xc = halved(x[:, j * 2 + b, :])
                            nc.vector.scalar_tensor_tensor(xc, job_out(b), 0.5, xc, ALU.mult,
                                                           ALU.add).then_inc(evac_done[b], 1)
                            if n < KM:
                                updated(2 * j + b)

                    if n == KM:
                        with dve.Fori(0, KM // 2 - 1) as j:
                            down(j, n * P)
                        down(KM // 2 - 1, KM * P)
                    else:
                        for j in range(KM // 2):
                            down(j, n * P if j < KM // 2 - 1 else (0 if f else KM * P))
                    half += KM // 2

            dve.sem_inc(evac_done[0], 1)
            dve.sem_inc(evac_done[1], 1)
            dve.sem_inc(lo_done, 2)
            dve.sem_inc(convb_ready, 2)
            dve.sem_inc(conva_ready, 1)
            dve.sem_inc(y_done, 1)
            dve.sem_inc(hs_new, 2)
            split_lo(0, 0)
            dve.wait_ge(x_in, 16 * KM)
            for c in range(KM):
                accumulate(Q_FFN1 + c, c % 2, c == 0)
                xa_low(S_FFN1 + c, x[:, c], 0, c)

            def norm_ffn1():
                variance(N_FFN1, DM, RMS_EPS)
                newton(0)

            ffn(0, norm_ffn1, lambda c: accumulate(Q_MIX + c, c % 2, c == 0))
            variance(N_MIX, DM, RMS_EPS)
            newton(1)
            for c in range(KM):
                nc.vector.tensor_tensor(sq[:, c % 2], x[:, c], rstd[:], ALU.mult).then_inc(nin_ready, 1)
                dve.wait_ge(nin_ready, c + 1)
                xa_low(S_MIX + c, sq[:, c % 2], 1, c)
            dve.wait_ge(spilled, 16 * KM)
            nc.vector.memset(ext_a[:, 0:HA], 0.0).then_inc(cleared, 1)
            nc.vector.memset(ext_b[:, :, 0:HB], 0.0).then_inc(cleared, 1)
            nc.vector.memset(yb[:], 0.0).then_inc(cleared, 1)
            dve.wait_ge(cleared, 3)
            dve.wait_ge(wdt_split, 1)
            nc.vector.tensor_tensor(wdt_lo[:], wdt_raw[:], wdt_hi[:].bitcast(F32), ALU.subtract).then_inc(wdt_lo_ready, 1)

            def by_tile(ap):
                return ap.rearrange("p (t h) -> p t h", t=NT)

            dve.wait_ge(dt_mm, 1)
            dve.wait_ge(wdt_in, 48)
            nc.vector.tensor_tensor(by_tile(dts[:, 0]), by_tile(pc[:, 0:NT * H]),
                                    dt_par[:, 0].unsqueeze(1).broadcast_to([P, NT, H]), ALU.add).then_inc(dt_dve, 1)
            dve.wait_ge(dt_act, 2)
            nc.vector.tensor_scalar(dts[:, 2], dts[:, 1], 1.0, None, ALU.add).then_inc(dt_dve, 1)
            dve.wait_ge(dt_dve, 2)
            nc.vector.scalar_tensor_tensor(dts[:, 4], dts[:, 2], 1.0, dts[:, 1], ALU.subtract,
                                           ALU.subtract).then_inc(dt_dve, 1)
            nc.vector.reciprocal(dts[:, 5], dts[:, 2]).then_inc(dt_dve, 1)
            dve.wait_ge(dt_dve, 4)
            nc.vector.tensor_tensor(dts[:, 4], dts[:, 4], dts[:, 5], ALU.mult).then_inc(dt_dve, 1)
            dve.wait_ge(dt_dve, 5)
            dve.wait_ge(dt_act, 4)
            nc.vector.tensor_tensor(dts[:, 3], dts[:, 3], dts[:, 4], ALU.subtract).then_inc(dt_dve, 1)
            dve.wait_ge(dt_dve, 6)
            nc.vector.scalar_tensor_tensor(tok[:, 0].rearrange("p t h -> p (t h)"), dts[:, 0], 0.0, dts[:, 3],
                                           ALU.max, ALU.add).then_inc(dt_dve, 1)
            dve.wait_ge(dt_dve, 7)
            nc.vector.scalar_tensor_tensor(by_tile(dts[:, 1]), tok[:, 0], -1.0,
                                           dt_par[:, 2].unsqueeze(1).broadcast_to([P, NT, H]),
                                           ALU.mult, ALU.mult).then_inc(dt_dve, 1)
            dve.wait_ge(cum_copied, 3)
            nc.vector.tensor_tensor(tok[:, 2], by_tile(pa[:, 256:256 + NT * H]), tok[:, 1],
                                    ALU.subtract).then_inc(tok_done, 1)
            dve.wait_ge(tok_done, 2)
            nc.vector.tensor_tensor(tok[:, 2], tok[:, 2], tok[:, 0], ALU.mult).then_inc(tok_done, 1)

            def group(g):
                def at(k):
                    return MIX_HALF + g * (GJ // 2) + k // 2, k % 2

                def evacuated(k):
                    half, b = at(k)
                    dve.wait_ge(evac_done[b], half + 2)

                def param(column):
                    return parg[:, column:column + 1]

                def tap(j, w0, bias, src, dst, ins_prev):
                    if j == 0:
                        return nc.vector.tensor_scalar(dst, src, param(w0), param(bias), ALU.mult, ALU.add)
                    return nc.vector.scalar_tensor_tensor(dst, src, param(w0 + j), dst, ALU.mult, ALU.add)

                def conv_xbc(k):
                    s, m = k % 2, NX * g + k
                    dve.wait_ge(extb_ready, 5 * m + 5)
                    evacuated(k)
                    dve.wait_ge(xbc_ready, m + 1)
                    w0 = P_CB + k * (KB + 1)
                    for j in range(KB):
                        if j:
                            dve.wait_ge(tap_b, (2 * KB - 1) * m + 2 * j - 1)
                        tap(j, w0, w0 + KB, ext_b[:, s, j:j + TP], conv_b[:, s, 0:TP], None).then_inc(tap_b, 1)
                        if j:
                            dve.wait_ge(tap_b, (2 * KB - 1) * m + 2 * j)
                        tap(j, w0, w0 + KB, seqs(ext_b[:, s, EB:])[:, :, j:j + TS], seqs(conv_b[:, s, TP:]),
                            None).then_inc(tap_b if j < KB - 1 else convb_ready, 1)

                def glu(k, c):
                    evacuated(k - 1)
                    dve.wait_ge(conva_ready, 2 * g + c + 1)
                    job_ended(*at(k))
                    b = k % 2
                    nc.vector.tensor_tensor(ext_a[:, HA:HA + TH], psj[:, b, 0, 0:TH], sig[:, 0:TH],
                                            ALU.mult).then_inc(u_part, 1)
                    nc.vector.tensor_tensor(ext_a[:, HA + TH:EA], psj[:, b, 1, 0:TP - TH], sig[:, TH:TP],
                                            ALU.mult).then_inc(u_part, 1)
                    nc.vector.tensor_tensor(seqs(ext_a[:, EA:])[:, :, HA:], seqs(psj[:, b, 1, TP - TH:TH]),
                                            seqs(sig[:, TP:T]), ALU.mult).then_inc(evac_done[b], 1)

                def conv_glu(k, c):
                    if k not in TAPS[c]:
                        return
                    m, n = 2 * g + c, 2 * KA - 1
                    start = sum(taps for job, taps in TAPS[c].items() if job < k)
                    w0 = P_CA + c * (KA + 1)
                    if start == 0:
                        evacuated((J_U0, J_U1)[c] + 1)
                        dve.wait_ge(u_part, 2 * m + 2)
                        dve.wait_ge(halo_a_in, 16 * m + 16)
                    for j in range(start, start + TAPS[c][k]):
                        if j:
                            dve.wait_ge(tap_a, n * m + 2 * j - 1)
                        tap(j, w0, w0 + KA, ext_a[:, j:j + TP], v[:, m, 0:TP], None).then_inc(tap_a, 1)
                        if j:
                            dve.wait_ge(tap_a, n * m + 2 * j)
                        tap(j, w0, w0 + KA, seqs(ext_a[:, EA:])[:, :, j:j + TS], seqs(v[:, m, TP:T]),
                            None).then_inc(tap_a if j < KA - 1 else conva_ready, 1)

                def heads(ap):
                    return ap.rearrange("p (h q) -> p h q", h=HG)

                def over_width(ap, width):
                    return ap.unsqueeze(2).broadcast_to([P, ap.shape[1], width])

                def over_heads(ap):
                    return ap.unsqueeze(1).broadcast_to([P, HG, ap.shape[1]])

                def state(t):
                    dve.wait_ge(s_mm, LAST * g + t + 2)
                    if t == 0:
                        dve.wait_ge(stored, g + 1)
                        nc.vector.tensor_copy(h_pr[:], pa).then_inc(state_ready, 1)
                        return
                    nc.vector.tensor_tensor(heads(h_pr[:]), heads(h_pr[:]), over_width(el[:, t % 2, :, 0], PD),
                                            ALU.mult).then_inc(state_step, 1)
                    dve.wait_ge(state_step, (LAST - 1) * g + t)
                    nc.vector.tensor_tensor(h_pr[:], h_pr[:], pa, ALU.add).then_inc(state_ready, 1)

                def prepare(t):
                    n = NT * g + t
                    dve.wait_ge(turned, n + 1)
                    nc.vector.tensor_tensor(heads(xdt[:]), heads(pa), over_width(tokg[:, 0, t], PD),
                                            ALU.mult).then_inc(xdt_ready, 1)
                    nc.vector.tensor_tensor(heads(xtl[:]), heads(pa), over_width(tokg[:, 2, t], PD),
                                            ALU.mult).then_inc(xdt_ready, 1)
                    nc.vector.tensor_tensor(cbm[:], pb[:, NS:NS + P], const[:, TRI if t < LAST else TRI_S],
                                            ALU.mult).then_inc(cbm_ready, 1)
                    dve.wait_ge(dec_ready, 2 * n + 2)
                    dve.wait_ge(cbm_ready, n + 1)
                    nc.vector.tensor_tensor(mdec[:], acb[:, t % 2], over_heads(cbm[:]), ALU.mult).then_inc(m_ready, 1)
                    if t == LAST:
                        dve.wait_ge(btok_ready, n + 1)
                        nc.vector.tensor_tensor(acb[:, 1], over_heads(btok[:]), over_width(bmask[:], NS),
                                                ALU.mult).then_inc(bm_ready, 1)

                def y_out(t):
                    steps = 24 * g + (0 if t == 0 else 5 * t - 1)
                    yt = y[:, :, t * P:(t + 1) * P]
                    pcv, pdv = (ap[:].rearrange("p (c i) -> p c i", c=GC) for ap in (pc, pd))
                    dve.wait_ge(y_mm, NT * g + t + 1)
                    if t == 0:
                        nc.vector.tensor_copy(yt, pcv).then_inc(y_step, 1)
                        steps += 1
                    else:
                        nc.vector.tensor_tensor(yt, pdv, ach[:, t % 2], ALU.mult).then_inc(y_step, 1)
                        dve.wait_ge(y_step, steps + 1)
                        nc.vector.tensor_tensor(yt, yt, pcv, ALU.add).then_inc(y_step, 1)
                        steps += 2
                    dve.wait_ge(y_step, steps)
                    for c in range(GC):
                        nc.vector.scalar_tensor_tensor(
                            yt[:, c], xs[:, c, t * P:(t + 1) * P], param(P_D + c), yt[:, c], ALU.mult,
                            ALU.add).then_inc(y_step if c < GC - 1 else y_done, 1)

                def sample_states():
                    for b in range(NB):
                        m = NB * g + b
                        hs = h_smp[:, b % 2]
                        dve.wait_ge(hs_mm, m + 1)
                        nc.vector.tensor_tensor(heads(hs), heads(hs), over_width(el[:, 0, :, b], PD),
                                                ALU.mult).then_inc(hs_step, 1)
                        dve.wait_ge(hs_step, m + 1)
                        nc.vector.tensor_tensor(hs, hs, (pa, pb)[b % 2], ALU.add).then_inc(hs_new, 1)

                dve.wait_ge(parg_ready, g + 1)
                for k in range(GJ):
                    split_lo(*at(k + 1), KM * P if k + 1 < J_O or k + 1 == GJ else GC * P)
                    if k < NX:
                        conv_xbc(k)
                    if k == J_U0 + 1:
                        dve.wait_ge(tokg_ready, g + 1)
                        prepare(0)
                        glu(k, 0)
                    if J_Z <= k < J_U1:
                        t = k - J_Z + 1
                        state(t - 1)
                        prepare(t)
                        y_out(t - 1)
                    if k == J_U1:
                        sample_states()
                        y_out(LAST)
                        dve.wait_ge(y_done, NT * g + NT + 1)
                        dve.wait_ge(y_step, 24 * g + 24)
                        evacuated(J_Z + GC - 2)
                        evacuated(J_Z + GC - 1)
                        for c in range(GC):
                            nc.vector.tensor_tensor(y[:, c], y[:, c], z[:, c], ALU.mult).then_inc(gz_ready, 1)
                        for c in range(GC):
                            accumulate(Q_GROUP + GC * g + c, c % 2, c == 0)
                            dve.wait_ge(gnhi_ready, GC * g + c + 1)
                            nc.vector.scalar_tensor_tensor(gn_lo[:, c], y[:, c], param(P_N + c),
                                                           gn_hi[:, c].bitcast(F32), ALU.mult,
                                                           ALU.subtract).then_inc(gnlo_ready, 1)
                    if k == J_U1 + 1:
                        variance(N_GROUP + g, GC * P, RMS_EPS)
                    conv_glu(k, 0)
                    if k == J_U1 + 1:
                        glu(k, 1)
                        newton(2 + g)
                    if k >= J_O:
                        half, b = at(k)
                        c = k - J_O
                        job_ended(half, b)
                        nc.vector.tensor_tensor(halved(y[:, c % 2]), job_out(b), halved(rstd[:]),
                                                ALU.mult).then_inc(evac_done[b], 1)
                        evacuated(k)
                        nc.vector.tensor_tensor(yb[:, c], yb[:, c], y[:, c % 2], ALU.add).then_inc(yb_ready, 1)
                    conv_glu(k, 1)

            with dve.Fori(0, G) as g:
                group(g)

            half = GATE_HALF
            dve.wait_ge(tap_a, (2 * KA - 1) * KM)
            dve.wait_ge(conva_ready, KM + 1)
            for c in range(KM):
                split_lo(half + (c + 1) // 2, (c + 1) % 2)
                if c == 0:
                    nc.vector.tensor_tensor(acc[:], v[:, 0], v[:, 1], ALU.add).then_inc(vsum_step, 1)
                    for i in range(2, KM):
                        dve.wait_ge(vsum_step, i - 1)
                        nc.vector.tensor_tensor(acc[:], acc[:], v[:, i], ALU.add).then_inc(vsum_step, 1)
                if c == 3:
                    dve.wait_ge(sum_ready, N_MEAN + 1)
                    nc.vector.tensor_scalar(halved(var), pab[:, :, 0:TH], 1.0 / DM, None, ALU.mult).then_inc(vsum_step, 1)
                    dve.wait_ge(vsum_step, KM)
                    for i in range(KM):
                        nc.vector.tensor_tensor(v[:, i], v[:, i], var, ALU.subtract).then_inc(vc_ready, 1)
                    for i in range(KM):
                        accumulate(Q_LN + i, i % 2, i == 0)
            variance(N_LN, DM, LN_EPS)
            newton(6)
            half += KM // 2
            dve.wait_ge(yb_ready, KM * G)
            for c in range(KM):
                split_lo(half + (c + 1) // 2, (c + 1) % 2)
                nc.vector.tensor_tensor(v[:, c], v[:, c], rstd[:], ALU.mult).then_inc(nin_ready, 1)
                dve.wait_ge(evac_done[c % 2], half + c // 2 + 2)
                nc.vector.tensor_tensor(yb[:, c], yb[:, c], gate_b[:, c % 2], ALU.mult).then_inc(gb_used, 1)
            half += KM // 2
            for c in range(KM):
                dve.wait_ge(xhi_ready, S_LN + c + 1)
                nc.vector.tensor_tensor(xa_lo[:, c], v[:, c], xa_hi[:, c].bitcast(F32), ALU.subtract).then_inc(xlo_ready, 1)
            dve.wait_ge(gb_used, KM)
            for c in range(KM):
                b = c % 2
                split_lo(half + (c + 1) // 2, (c + 1) % 2)
                job_ended(half + c // 2, b)
                nc.vector.tensor_tensor(halved(prod[:]), job_out(b), halved(gate_a[:, c]), ALU.mult).then_inc(evac_done[b], 1)
                dve.wait_ge(evac_done[b], half + c // 2 + 2)
                nc.vector.tensor_tensor(yb[:, c], yb[:, c], prod[:], ALU.add).then_inc(merge_ready, 1)
                dve.wait_ge(mhi_ready, c + 1)
                nc.vector.tensor_tensor(merged_lo[:, c], yb[:, c], merged_hi[:, c].bitcast(F32),
                                        ALU.subtract).then_inc(mlo_ready, 1)
            half += KM // 2
            dve.wait_ge(x_back, 16 * KM)
            for c in range(KM):
                b = c % 2
                split_lo(half + (c + 1) // 2, (c + 1) % 2)
                job_ended(half + c // 2, b)
                nc.vector.tensor_tensor(halved(x[:, c]), job_out(b), halved(x[:, c]), ALU.add).then_inc(evac_done[b], 1)
                accumulate(Q_FFN2 + c, b, c == 0)
                xa_low(S_FFN2 + c, x[:, c], 2, c)

            def norm_ffn2():
                variance(N_FFN2, DM, RMS_EPS)
                newton(7)

            ffn(1, norm_ffn2, lambda c: accumulate(Q_OUT + c, c % 2, c == 0))
            variance(N_OUT, DM, RMS_EPS)
            newton(8)
            for c in range(KM):
                nc.vector.scalar_tensor_tensor(x[:, c], x[:, c], gains[:, 3, c:c + 1], rstd[:], ALU.mult,
                                               ALU.mult).then_inc(out_ready, 1)

        @block.tensor
        def _(pe):
            def job(half, b, chunks, in_hi, in_lo, before=None):
                pe.wait_ge(lo_done, 2 * half + b + 3)
                pe.wait_ge(evac_done[b], half + 1)
                for k in range(chunks):
                    if before:
                        before(k)
                    cols = slice(k * P, (k + 1) * P)
                    for n, (w, act_in) in enumerate(((w_hi, in_hi), (w_hi, in_lo), (w_lo, in_hi))):
                        for u in range(2):
                            last = nc.tensor.matmul(psj[:, b, u, 0:TH], w[:, b, cols],
                                                    act_in[:, k, u * TH:(u + 1) * TH],
                                                    start=(k == 0 and n == 0), stop=(k == chunks - 1 and n == 2))
                last.then_inc(job_done, 1)

            def token_sums():
                for u in range(2):
                    last = nc.tensor.matmul(pab[:, u, 0:TH], const[:, ONES], acc[:, u * TH:(u + 1) * TH],
                                            start=True, stop=True)
                last.then_inc(sum_ready, 1)

            def ffn(f):
                half, q0 = f * FFN2_HALF, NFF * f

                def first_input(k):
                    m = (S_FFN1, S_FFN2)[f] + k
                    pe.wait_ge(xlo_ready, m + 1)
                    if k == KM - 1:
                        pe.wait_ge(acc_ready, (Q_FFN1, Q_FFN2)[f] + KM)
                        token_sums()

                for p, n in enumerate(PARTS):
                    if p == 0:
                        job(half, 0, KM, xa_hi, xa_lo, first_input)
                        job(half, 1, KM, xa_hi, xa_lo)
                    with pe.Fori(1 if p == 0 else 0, n) as i:
                        for b in range(2):
                            job(half + i, b, KM, xa_hi, xa_lo)
                    half += n

                    def hidden(k, q0=q0):
                        pe.wait_ge(hlo_ready, q0 + k + 1)

                    job(half, 0, n, h_hi, h_lo, hidden)
                    job(half, 1, n, h_hi, h_lo)
                    with pe.Fori(1, KM // 2) as j:
                        for b in range(2):
                            job(half + j, b, n, h_hi, h_lo)
                    half += KM // 2
                    q0 += n

            pe.sem_inc(job_done, 2)
            pe.sem_inc(s_mm, 1)
            pe.wait_ge(par_in, 64)
            ffn(0)
            pe.wait_ge(acc_ready, Q_MIX + KM)
            token_sums()
            pe.wait_ge(wdt_lo_ready, 1)
            pe.wait_ge(xlo_ready, S_MIX + KM)
            for t in range(NT):
                tokens = slice(t * P, (t + 1) * P)
                for k in range(KM):
                    cols = slice(k * H, (k + 1) * H)
                    for n, (a, w) in enumerate(((xa_hi, wdt_hi), (xa_lo, wdt_hi), (xa_hi, wdt_lo))):
                        last = nc.tensor.matmul(pc[:, t * H:(t + 1) * H], a[:, k, tokens], w[:, cols],
                                                start=(k == 0 and n == 0), stop=(k == KM - 1 and n == 2))
            last.then_inc(dt_mm, 1)
            pe.wait_ge(dt_dve, 8)
            for t in range(NT):
                tri, ones = (TRI, ONES) if t < LAST else (TRI_S, BLK_S)
                da = dts[:, 1, t * H:(t + 1) * H]
                nc.tensor.matmul(pa[:, t * H:(t + 1) * H], const[:, tri], da, start=True, stop=True)
                nc.tensor.matmul(pa[:, 256 + t * H:256 + (t + 1) * H], const[:, ones], da, start=True, stop=True)
                out = pb[0:H, t * P:(t + 1) * P] if t < LAST else pc[0:H, 0:P]
                last = nc.tensor.matmul(out, da, const[:, tri], start=True, stop=True)
            last.then_inc(cum_mm, 1)

            def group(g):
                def run(k, before=None):
                    half, b = MIX_HALF + g * (GJ // 2) + k // 2, k % 2
                    if k < J_O:
                        job(half, b, KM, xa_hi, xa_lo, before)
                    else:
                        job(half, b, GC, gn_hi, gn_lo, before)

                def turn(t):
                    cols = slice(t * P, (t + 1) * P)
                    if t == 0:
                        pe.wait_ge(tokg_ready, g + 1)
                        pe.wait_ge(xbc_ready, NX * g + NX + 2)
                        pe.wait_ge(var_ready, g + 2)
                    else:
                        pe.wait_ge(state_ready, LAST * g + t)
                    for c in range(GC):
                        nc.tensor.transpose(pa[:, c * P:(c + 1) * P], xs[:, c, cols], const[:, IDENT])
                    nc.tensor.transpose(pb[:, 0:P], bc[:, 0, cols], const[:, IDENT])
                    nc.tensor.matmul(pb[:, P:2 * P], bc[:, 0, cols], bc[:, 1, cols], start=True,
                                     stop=True).then_inc(turned, 1)

                def tile(t):
                    n = NT * g + t
                    cols = slice(t * P, (t + 1) * P)
                    pe.wait_ge(xdt_ready, 2 * n + 2)
                    pe.wait_ge(m_ready, n + 1)
                    pe.wait_ge(y_done, n + 1)
                    for c in range(GC):
                        for e in range(2):
                            hh = 2 * c + e
                            last = nc.tensor.matmul(pc[e * PD:(e + 1) * PD, c * P:(c + 1) * P],
                                                    xdt[:, hh * PD:(hh + 1) * PD], mdec[:, hh], start=True, stop=True)
                    if t == 0:
                        last.then_inc(y_mm, 1)
                    elif t < LAST:
                        pe.wait_ge(state_ready, LAST * g + t)
                        for c in range(GC):
                            last = nc.tensor.matmul(pd[:, c * P:(c + 1) * P], h_pr[:, c * P:(c + 1) * P],
                                                    bc[:, 1, cols], start=True, stop=True)
                        last.then_inc(y_mm, 1)
                    if t < LAST:
                        pe.wait_ge(btok_ready, n + 1)
                        nc.tensor.matmul(pa, btok[:], xtl[:], start=True, stop=True).then_inc(s_mm, 1)
                        return
                    pe.wait_ge(bm_ready, g + 1)
                    for b in range(NB):
                        m = NB * g + b
                        pe.wait_ge(hs_in[b % 2], 64 * g + 16 * (b // 2) + 16)
                        for c in range(GC):
                            out = pd[:, c * P + b * TS:c * P + (b + 1) * TS]
                            last = nc.tensor.matmul(out, h_smp[:, b % 2, c * P:(c + 1) * P],
                                                    bc[:, 1, TP + b * TS:TP + (b + 1) * TS], start=True, stop=True)
                        if b == NB - 1:
                            last.then_inc(y_mm, 1)
                        pe.wait_ge(hs_new, m + 1)
                        nc.tensor.matmul((pa, pb)[b % 2], acb[:, 1, b], xtl[:], start=True, stop=True).then_inc(hs_mm, 1)

                for k in range(GJ):
                    t = k - (J_U0 + 1)
                    if 0 <= t < NT:
                        run(k, lambda i, t=t: turn(t) if i == KM // 2 else None)
                        tile(t)
                    elif k == J_U1 + 1:
                        def norm_sum(i):
                            if i == KM // 2:
                                pe.wait_ge(acc_ready, Q_GROUP + GC * (g + 1))
                                pe.wait_ge(hs_new, NB * g + NB + 2)
                                token_sums()
                        run(k, norm_sum)
                    elif k == J_O:
                        run(k, lambda i: pe.wait_ge(gnlo_ready, GC * g + i + 1))
                    else:
                        run(k)

            with pe.Fori(0, G) as g:
                group(g)

            half = GATE_HALF
            for c in range(KM):
                job(half + c // 2, c % 2, KM, xa_hi, xa_lo)
                if c == 2:
                    pe.wait_ge(vsum_step, KM - 1)
                    token_sums()
                if c == 5:
                    pe.wait_ge(acc_ready, Q_LN + KM)
                    token_sums()
            half += KM // 2
            with pe.Fori(0, KM // 2) as j:
                for b in range(2):
                    job(half + j, b, KM, xa_hi, xa_lo)
            half += KM // 2
            job(half, 0, KM, xa_hi, xa_lo, lambda k: pe.wait_ge(xlo_ready, S_LN + k + 1))
            job(half, 1, KM, xa_hi, xa_lo)
            with pe.Fori(1, KM // 2) as j:
                for b in range(2):
                    job(half + j, b, KM, xa_hi, xa_lo)
            half += KM // 2
            job(half, 0, KM, merged_hi, merged_lo, lambda k: pe.wait_ge(mlo_ready, k + 1))
            job(half, 1, KM, merged_hi, merged_lo)
            with pe.Fori(1, KM // 2) as j:
                for b in range(2):
                    job(half + j, b, KM, merged_hi, merged_lo)
            ffn(1)
            pe.wait_ge(acc_ready, Q_OUT + KM)
            token_sums()


NAMES = ("x", "w_gu", "w_down", "w_down_last", "w_mix", "w_ssm", "w_tail", "w_dt", "gains", "par", "halo_a", "halo_b",
         "dt_bias", "a_log", "h_sample", "const", "bmask")
OUTS = {"y": (KM, P, T), "new_a_prompt": (KM, P, HA), "new_a_sample": (KM, P, NB, HA),
        "new_b": (P, G, NX, HB + NB * HB), "new_h_prompt": (G, NS, HG * PD), "new_h_sample": (G, NB, NS, HG * PD)}


def lay_out(inp):
    import numpy as np

    a = {k: np.asarray(v) for k, v in inp.items()}

    def blocks(w):
        k, n = w.shape
        return np.ascontiguousarray(w.reshape(k // P, P, n // P, P).transpose(2, 1, 0, 3)).reshape(n // P, P, k)

    def columns(vec):
        return vec.reshape(-1, P).T

    out = {}
    xt = np.concatenate([a["x_prompt"].reshape(TP, DM), a["x_sample"].reshape(NB * TS, DM)], 0).T
    out["x"] = xt.reshape(KM, P, T)
    w_gu, w_down, w_last = [], [], []
    for f in ("ffn1", "ffn2"):
        w_gu.append(np.stack([blocks(a[f + "_w_gate"][0]), blocks(a[f + "_w_up"][0])], 1))
        down = a[f + "_w_down"][0]
        w_down.append(np.stack([blocks(down[p * DM:(p + 1) * DM]) for p in range(2)], 0))
        w_last.append(blocks(down[2 * DM:]))
    out["w_gu"] = np.stack(w_gu)
    out["w_down"] = np.stack(w_down).reshape(2, 2, KM // 2, 2, P, DM)
    out["w_down_last"] = np.stack(w_last).reshape(2, KM // 2, 2, P, PARTS[2] * P)
    w_in = a["w_in"][0]
    o_z, o_x = 2 * DM, 2 * DM + G * GC * P
    o_dt = o_x + G * NX * P
    o_g = o_dt + H
    wb = blocks(np.concatenate([w_in[:, :o_dt], w_in[:, o_g:]], 1))
    u0, z0, x0, g0 = 0, o_z // P, o_x // P, o_dt // P
    order = []
    for g in range(G):
        xbc = [x0 + g * GC + c for c in range(GC)] + [x0 + G * GC + g, x0 + G * GC + G + g]
        glu = [[KM + 2 * g + c, u0 + 2 * g + c] for c in range(2)]
        order.append(xbc + glu[0] + [z0 + g * GC + c for c in range(GC)] + glu[1])
    out["w_mix"] = wb[np.array(order)]
    out["w_ssm"] = np.stack([blocks(a["w_ssm_out"][0][g * GC * P:(g + 1) * GC * P]) for g in range(G)])
    out["w_tail"] = np.concatenate([wb[g0:g0 + 2 * KM], blocks(a["w_conv_a_out"][0]), blocks(a["w_out"][0])]
                                   ).reshape(2 * KM, 2, P, DM)
    out["w_dt"] = w_in[:, o_dt:o_g].reshape(KM, P, H).transpose(1, 0, 2).reshape(P, KM * H)
    out["gains"] = np.stack([columns(a[n].reshape(-1)) for n in
                             ("norm_ffn1", "norm_mix", "norm_ffn2", "norm_final", "ln_conv_g", "ln_conv_b")], 1)
    par = np.zeros((P, G, NPAR), np.float32)
    cb = np.concatenate([a["conv_b_w"][0], a["conv_b_b"]], 0).reshape(KB + 1, -1, P)
    ca = np.concatenate([a["conv_a_w"][0], a["conv_a_b"]], 0).reshape(KA + 1, -1, P)
    head_d = columns(np.repeat(a["d_skip"][0], PD))
    ng = columns(a["ssm_norm_g"][0])
    sb_ = a["state_conv_b"][0].reshape(NB, HB, -1, P)
    halo_b = np.zeros((P, G, NX, NB * HB), np.float32)
    for g in range(G):
        for k in range(NX):
            ch = g * GC + k if k < GC else G * GC + (k - GC) * G + g
            par[:, g, P_CB + k * (KB + 1):P_CB + (k + 1) * (KB + 1)] = cb[:, ch].T
            halo_b[:, g, k] = sb_[:, :, ch].transpose(2, 0, 1).reshape(P, NB * HB)
        for c in range(2):
            par[:, g, P_CA + c * (KA + 1):P_CA + (c + 1) * (KA + 1)] = ca[:, 2 * g + c].T
        par[:, g, P_D:P_D + GC] = head_d[:, g * GC:(g + 1) * GC]
        par[:, g, P_N:P_N + GC] = ng[:, g * GC:(g + 1) * GC]
    out["par"], out["halo_b"] = par, halo_b
    out["halo_a"] = a["state_conv_a"][0].reshape(NB, HA, KM, P).transpose(2, 3, 0, 1)
    out["dt_bias"], out["a_log"] = a["dt_bias"][0], a["a_log"][0]
    out["h_sample"] = a["state_ssm"][0].reshape(NB, G, HG * PD, NS).transpose(1, 0, 3, 2)
    i = np.arange(P)
    causal, same = i[:, None] <= i[None, :], i[:, None] // TS == i[None, :] // TS
    out["const"] = np.stack([causal, causal & same, np.ones((P, P), bool), same, i[:, None] == i[None, :]], 1
                            ).astype(np.float32)
    out["bmask"] = (i[:, None] // TS == np.arange(NB)[None, :]).astype(np.float32)
    return {k: np.ascontiguousarray(out[k]) for k in NAMES}


def bring_back(r):
    import numpy as np

    y = r["y"].reshape(DM, T).T
    na_p = r["new_a_prompt"].transpose(2, 0, 1).reshape(1, 1, HA, DM)
    na_s = r["new_a_sample"].transpose(2, 3, 0, 1).reshape(1, NB, HA, DM)
    nb = r["new_b"]
    nb = np.concatenate([nb[:, :, :GC].reshape(P, G * GC, -1), nb[:, :, GC], nb[:, :, GC + 1]], 1)
    nb = nb.transpose(2, 1, 0).reshape(HB + NB * HB, -1)
    hp = r["new_h_prompt"].transpose(0, 2, 1).reshape(1, 1, H, PD, NS)
    hs = r["new_h_sample"].transpose(1, 0, 3, 2).reshape(1, NB, H, PD, NS)
    outs = (y[:TP].reshape(1, TP, DM), y[TP:].reshape(NB, TS, DM), na_p, nb[:HB].reshape(1, 1, HB, -1), hp,
            na_s, nb[HB:].reshape(1, NB, HB, -1), hs)
    return tuple(np.ascontiguousarray(o) for o in outs)


def kernel(**inputs):
    import concourse.bacc as _bacc
    from concourse.bass_utils import run_bass_kernel_spmd as _run

    nc = _bacc.Bacc("TRN2", target_bir_lowering=False, num_devices=1)
    laid = lay_out(inputs)
    d = {n: nc.dram_tensor(f"in_{n}", a.shape, mybir.dt.from_np(a.dtype), kind="ExternalInput").ap()
         for n, a in laid.items()}
    for n, shape in OUTS.items():
        d[n] = nc.dram_tensor(f"out_{n}", shape, F32, kind="ExternalOutput").ap()
    build(nc, d)
    r = _run(nc, [{f"in_{n}": a for n, a in laid.items()}], core_ids=[0])
    return bring_back({n: r.results[0][f"out_{n}"] for n in OUTS})
```

```python
from contextlib import ExitStack

import concourse.bass as bass
from concourse import mybir

F32 = mybir.dt.float32
F32R = mybir.dt.float32r
ALU = mybir.AluOpType
ACT = mybir.ActivationFunctionType

P = 128
TP, NB, TS = 512, 8, 16
T = TP + NB * TS
TH = T // 2
NT = T // P
LAST = NT - 1
DM = 1024
KM = DM // P
PARTS = (8, 8, 6)
NFF = sum(PARTS)
DFF = NFF * P
KA, KB = 31, 4
HA, HB = KA - 1, KB - 1
G, HG, PD, NS = 4, 8, 64, 128
H = G * HG
GC = HG * PD // P
NX = GC + 2
EA, EB = HA + TP, HB + TP
WA, WB = EA + NB * (HA + TS), EB + NB * (HB + TS)
RMS_EPS, LN_EPS = 1e-6, 1e-5

J_U0, J_Z, J_U1, J_O = NX, NX + 2, NX + 2 + GC, NX + 4 + GC
GJ = J_O + KM
TAPS = ({8.5: 3, 9.5: 4, 10.5: 4, 11.5: 4, 12: 9, 13.5: 2, 15: 1, 16: 1, 17: 1, 18: 1},
        dict(zip(range(19, GJ + 7), (1, 1, 2, 3, 3, 3, 3, 3, 3, 5))) | {GJ + 7.5: 3})
assert all(sum(taps.values()) == KA - 1 for taps in TAPS)
ON_SCALAR = (6, 7)
LN_CHUNKS = {4: (0, 1, 2), 5: (3, 4, 5), 6: (6, 7)}

FFN_HALVES = sum(n + KM // 2 for n in PARTS)
MIX_HALF = FFN_HALVES
GATE_HALF = MIX_HALF + G * GJ // 2
FFN2_HALF = GATE_HALF + 4 * KM // 2

P_CB, P_CA = 0, NX * (KB + 1)
P_D = P_CA + 2 * (KA + 1)
P_N = P_D + GC
NPAR = P_N + GC
TRI, TRI_S, ONES, BLK_S, IDENT = range(5)
N_FFN1, N_MIX, N_GROUP, N_MEAN, N_LN, N_FFN2, N_OUT = 0, 1, 2, 6, 7, 8, 9
Q_FFN1, Q_MIX, Q_GROUP, Q_LN, Q_FFN2, Q_OUT = 0, KM, 2 * KM, 2 * KM + G * GC, 3 * KM + G * GC, 4 * KM + G * GC
S_FFN1, S_MIX, S_LN, S_FFN2 = 0, KM, 2 * KM, 3 * KM


def build(nc, d):
    with ExitStack() as ctx:
        def sb(name, shape, dt=F32, stack=ctx):
            return stack.enter_context(nc.sbuf_tensor(name, shape, dt))

        def sem(name):
            return ctx.enter_context(nc.semaphore(name))

        xa_hi = sb("xa_hi", [P, KM, T], F32R)
        xa_lo = sb("xa_lo", [P, KM, T], F32R)
        w_raw = sb("w_raw", [P, 2, KM * P])
        w_hi = sb("w_hi", [P, 2, KM * P], F32R)
        w_lo = sb("w_lo", [P, 2, KM * P], F32R)
        const = sb("const", [P, 5, P])
        parc = sb("parc", [P, KA + 1])
        bmask = sb("bmask", [P, NB])
        gains = sb("gains", [P, 6, KM])
        acc = sb("acc", [P, T])
        sq = sb("sq", [P, 2, T])
        pair = sb("pair", [P, 2, T])
        var, rsq0 = pair[:, 0], pair[:, 1]
        conv_b = pair
        rstd = sb("rstd", [P, T])
        par = sb("par", [P, G, NPAR])
        parg = sb("parg", [P, NPAR])
        halo_b = sb("halo_b", [P, G, NX, NB * HB])
        new_b = sb("new_b", [P, G, NX, HB + NB * HB])
        tok = sb("tok", [P, 3, NT, H])
        tokg = sb("tokg", [P, 3, NT, HG])
        dt_par = sb("dt_par", [P, 3, H])

        def here(*tensors):
            with ExitStack() as stack:
                return [sb(*t, stack=stack) for t in tensors]

        h_hi, h_lo = here(("h_hi", [P, KM, T], F32R), ("h_lo", [P, KM, T], F32R))
        merged_hi, = here(("merged_hi", [P, KM, T], F32R))
        v = sb("v", [P, KM, T])
        yb = sb("yb", [P, KM, T])
        x, gate_s, silu_g, up_s, hid = here(
            ("x", [P, KM, T]), ("gate_s", [P, T]), ("silu_g", [P, T]), ("up_s", [P, T]), ("hid", [P, T]))
        _, gate_a, gate_b, prod = here(
            ("x_place", [P, KM, T]), ("gate_a", [P, KM, T]), ("gate_b", [P, 2, T]), ("prod", [P, T]))
        _, merged_lo = here(("x_place2", [P, KM, T]), ("merged_lo", [P, KM, T], F32R))
        ext_b = sb("ext_b", [P, 2, WB])
        ext_a = sb("ext_a", [P, 2, WA])
        sig = sb("sig", [P, T])
        h_pr = sb("h_pr", [P, HG * PD])
        bc = sb("bc", [P, 2, T])
        gn_hi, = here(("gn_hi", [P, GC, T], F32R))
        xs = sb("xs", [P, GC, T])
        gn_lo, = here(("gn_lo", [P, GC, T], F32R))
        mdec = sb("mdec", [P, HG, P])
        acb = sb("acb", [P, 2, HG, P])
        z = sb("z", [P, GC, T])
        cum_sb, wdt_raw, wdt_hi, wdt_lo = here(
            ("cum_sb", [P, T]), ("wdt_raw", [P, KM * H]), ("wdt_hi", [P, KM * H], F32R), ("wdt_lo", [P, KM * H], F32R))
        y = sb("y", [P, GC, T])
        dts, = here(("dts", [P, 6, NT * H]))
        xdt = sb("xdt", [P, HG * PD])
        xtl = sb("xtl", [P, HG * PD])
        btok = sb("btok", [P, NS])
        cbm = sb("cbm", [P, P])
        ach = sb("ach", [P, 2, GC, P])
        el = sb("el", [P, 2, HG, NB])

        b_one = [ach[:, 1, b] for b in range(NB // 2)] + [acb[:, 1, b] for b in range(NB // 2, NB)]
        width = HG * PD
        in_ext = [ext_b[:, s, HB:HB + width] for s in range(2)]
        old_h = [rstd[:, 0:width], sig[:, 0:width], *(sq[:, s, 0:width] for s in range(2)),
                 *(conv_b[:, s, 0:width] for s in range(2)), *in_ext]
        z_flat = z[:].rearrange("p c t -> p (c t)")
        new_h = [old_h[0], *(z_flat[:, i * width:(i + 1) * width] for i in range(NB - 3)), *in_ext]
        x_spill = nc.dram_tensor("x_spill", (KM, P, T), F32).ap()
        cum_dram = nc.dram_tensor("cum_dram", (G, GC, 2, T), F32).ap()
        psj = ctx.enter_context(nc.psum_tensor("psj", [P, 2, 2, 512], F32))
        pab = ctx.enter_context(nc.psum_tensor("pab", [P, 2, 512], F32))
        pc = ctx.enter_context(nc.psum_tensor("pc", [P, 512], F32))
        pd = ctx.enter_context(nc.psum_tensor("pd", [P, 512], F32))
        pa, pb = pab[:, 0], pab[:, 1]

        def job_out(b):
            return psj[:, b, :, 0:TH]

        def halved(ap):
            return ap.rearrange("p (u t) -> p u t", u=2)

        def seqs(ap):
            return ap.rearrange("p (b t) -> p b t", b=NB)

        raw_in = [sem("raw_in0"), sem("raw_in1")]
        hi_done = sem("hi_done")
        lo_done = sem("lo_done")
        job_done = sem("job_done")
        evac_done = [sem("evac0"), sem("evac1")]
        const_in, par_in = sem("const_in"), sem("par_in")
        x_in = [sem(f"x_in{c}") for c in range(KM)]
        silu_ready = sem("silu_ready")
        hid_ready, hhi_ready, hlo_ready = sem("hid_ready"), sem("hhi_ready"), sem("hlo_ready")
        sq_ready, acc_ready = sem("sq_ready"), sem("acc_ready")
        nin_ready = sem("nin_ready")
        vs_ready = sem("vs_ready")
        xhi_ready, xlo_ready = sem("xhi_ready"), sem("xlo_ready")
        sum_ready, var_ready, rsq_ready, rstd_ready = sem("sum_ready"), sem("var_ready"), sem("rsq_ready"), sem("rstd_ready")
        ln_step, newton_step = sem("ln_step"), sem("newton_step")
        spilled, x_back = sem("spilled"), sem("x_back")
        wdt_in, wdt_split, wdt_lo_ready, dt_mm = sem("wdt_in"), sem("wdt_split"), sem("wdt_lo_ready"), sem("dt_mm")
        dt_act, dt_dve, cum_mm = sem("dt_act"), sem("dt_dve"), sem("cum_mm")
        cum_copied, cum_out, tok_done = sem("cum_copied"), sem("cum_out"), sem("tok_done")
        cleared = sem("cleared")
        parg_ready, tokg_ready = sem("parg_ready"), sem("tokg_ready")
        extb_ready = sem("extb_ready")
        tap_b = sem("tap_b")
        convb_ready = sem("convb_ready")
        xbc_ready = sem("xbc_ready")
        halo_a_in = [sem("halo_a_in0"), sem("halo_a_in1")]
        u_part = sem("u_part")
        u_saved = sem("u_saved")
        tap_a = [sem("tap_a0"), sem("tap_a1")]
        conva_ready = [sem("conva_ready0"), sem("conva_ready1")]
        parc_ready = sem("parc_ready")
        newest_a = [sem("newest_a0"), sem("newest_a1")]
        z_ready = sem("z_ready")
        acb_in = [sem(f"acb_in{t}") for t in range(NT)]
        ach_in = [sem(f"ach_in{t}") for t in range(NT)]
        turned = sem("turned")
        btok_ready, xdt_ready, cbm_ready, m_ready = sem("btok_ready"), sem("xdt_ready"), sem("cbm_ready"), sem("m_ready")
        xtl_ready = sem("xtl_ready")
        dec_step, dec_ready, dech_ready = sem("dec_step"), sem("dec_ready"), sem("dech_ready")
        y_mm = sem("y_mm")
        s_mm = sem("s_mm")
        state_step, state_ready = sem("state_step"), sem("state_ready")
        y_step = sem("y_step")
        dx_ready = sem("dx_ready")
        y_done = sem("y_done")
        bm_ready = sem("bm_ready")
        hs_in = sem("hs_in")
        hs_mm, hs_step = sem("hs_mm"), sem("hs_step")
        hs_scalar = sem("hs_scalar")
        hs_new = sem("hs_new")
        hs_out = [sem("hs_out0"), sem("hs_out")]
        hp_out = sem("hp_out")
        stored = sem("stored")
        gz_ready = sem("gz_ready")
        gnhi_ready, gnlo_ready = sem("gnhi_ready"), sem("gnlo_ready")
        yo_step = sem("yo_step")
        yb_ready = sem("yb_ready")
        gb_ready, gb_used = sem("gb_ready"), sem("gb_used")
        vsum_step, vc_ready = sem("vsum_step"), sem("vc_ready")
        prod_step, merge_ready, mhi_ready, mlo_ready = sem("prod_step"), sem("merge_ready"), sem("mhi_ready"), sem("mlo_ready")
        out_ready, saved, y_saved = sem("out_ready"), sem("saved"), sem("y_saved")
        pool_passed = sem("pool_passed")

        def x_updated(eng, end_half, c):
            eng.wait_ge(evac_done[c % 2], end_half - KM // 2 + c // 2 + 2)

        block = ctx.enter_context(nc.Block())

        @block.sync
        def _(sp):
            def load(half, b, src, width=KM * P):
                sp.wait_ge(lo_done, 2 * half + b + 1)
                sp.dma_start(w_raw[:, b, 0:width], src).then_inc(raw_in[b], 16)

            def old_states(g, samples):
                for b in samples:
                    sp.dma_start(old_h[b], d["h_sample"][g, b]).then_inc(hs_in, 16)

            sp.dma_start(gains[:], d["gains"]).then_inc(const_in, 16)
            load(0, 0, d["w_gu"][0, 0, 0])
            for c in range(KM):
                sp.dma_start(x[:, c, :], d["x"][c]).then_inc(x_in[c], 16)
                if c == 0:
                    load(0, 1, d["w_gu"][0, 0, 1])
            half = 0
            for f in range(2):
                chunk = 0
                for p, n in enumerate(PARTS):
                    with sp.Fori(1 if half == 0 else 0, n) as i:
                        for b in range(2):
                            load(half + i, b, d["w_gu"][f, i + chunk, b])
                    half += n
                    chunk += n
                    w_down = d["w_down"][f, p] if n == KM else d["w_down_last"][f]
                    with sp.Fori(0, KM // 2) as j:
                        for b in range(2):
                            load(half + j, b, w_down[j, b], n * P)
                    half += KM // 2
                if f == 0:
                    with sp.Fori(0, G) as g:
                        for k in range(GJ):
                            src = d["w_mix"][g, k] if k < J_O else d["w_ssm"][g, k - J_O]
                            load(MIX_HALF + g * (GJ // 2) + k // 2, k % 2, src, KM * P if k < J_O else GC * P)
                            if k == 4:
                                sp.wait_ge(convb_ready, NX * g + 3)
                                old_states(g, (0, 2, 3))
                            if k == J_U0 + 3:
                                sp.wait_ge(xbc_ready, NX * g + NX + 2)
                                old_states(g, (4, 5, 6, 7))
                            if k == J_U0 + 4:
                                sp.wait_ge(evac_done[1], MIX_HALF + g * (GJ // 2) + J_U0 // 2 + 2)
                                old_states(g, (1,))
                    with sp.Fori(0, 2 * KM) as i:
                        for b in range(2):
                            load(GATE_HALF + i, b, d["w_tail"][i, b])
                    half = FFN2_HALF

            for c in range(KM):
                sp.wait_ge(out_ready, c + 1)
                sp.dma_start(d["y"][c], x[:, c, :]).then_inc(y_saved, 16)
            sp.wait_ge(y_saved, 16 * KM)

        @block.gpsimd
        def _(pool):
            pool.sem_inc(stored, 1)
            pool.dma_start(const[:], d["const"]).then_inc(par_in, 16)
            pool.wait_ge(x_in[KM - 1], 16)
            pool.dma_start(par[:], d["par"]).then_inc(par_in, 16)
            pool.dma_start(halo_b[:], d["halo_b"]).then_inc(par_in, 16)
            pool.dma_start(bmask[:], d["bmask"]).then_inc(par_in, 16)
            pool.dma_start(wdt_raw[:], d["w_dt"]).then_inc(wdt_in, 16)
            pool.dma_start(dt_par[:, 0], d["dt_bias"].partition_broadcast(P)).then_inc(wdt_in, 16)
            pool.dma_start(dt_par[:, 1], d["a_log"].partition_broadcast(P)).then_inc(wdt_in, 16)
            for c in range(KM):
                x_updated(pool, MIX_HALF, c)
                pool.dma_start(x_spill[c], x[:, c, :]).then_inc(spilled, 16)
            pool.wait_ge(cum_copied, 3)
            pool.dma_start(cum_dram.rearrange("g c e t -> (g c e) t"), cum_sb[0:H, :]).then_inc(cum_out, 16)
            pool.wait_ge(cum_out, 16)
            pool.wait_ge(cleared, 2)

            def group(g):
                def wait(semaphore, value):
                    pool.wait_ge(semaphore, value)
                    pool.sem_inc(pool_passed, 1)

                def tile(t):
                    cols = slice(t * P, (t + 1) * P)
                    if t >= 2:
                        wait(m_ready, NT * g + t - 1)
                    pool.dma_start(acb[:, t % 2], cum_dram[g].rearrange("c e t -> (c e) t")[:, cols]
                                   .partition_broadcast(P)).then_inc(acb_in[t], 16)
                    if t >= 2:
                        wait(y_done, NT * g + t)
                    for e in range(2):
                        pool.dma_start(ach[e * PD:(e + 1) * PD, t % 2], cum_dram[g, :, e, cols]
                                       .partition_broadcast(PD)).then_inc(ach_in[t], 16)

                def halo_a(c):
                    wait(conva_ready[c], g + 1)
                    pool.dma_start(seqs(ext_a[:, c, EA:])[:, :, 0:HA], d["halo_a"][2 * g + c]).then_inc(halo_a_in[c], 16)

                def save_a(c):
                    wait(halo_a_in[c], 16 * (g + 1))
                    wait(u_part, 2 * (2 * g + c + 1))
                    wait(evac_done[1], MIX_HALF + g * (GJ // 2) + (J_U0, J_U1)[c] // 2 + 2)
                    pool.dma_start(d["new_a_prompt"][2 * g + c], ext_a[:, c, TP:EA]).then_inc(u_saved, 16)
                    pool.dma_start(d["new_a_sample"][2 * g + c],
                                   seqs(ext_a[:, c, EA:])[:, :, TS:]).then_inc(u_saved, 16)

                wait(job_done, 2 * MIX_HALF + g * GJ + 2)
                tile(0)
                tile(1)
                halo_a(0)
                save_a(0)
                halo_a(1)
                for t in range(2, NT):
                    tile(t)
                wait(state_ready, LAST * g + LAST)
                pool.dma_start(d["new_h_prompt"][g], h_pr[:]).then_inc(hp_out, 16)
                for b in range(NB):
                    wait(hs_new, NB * g + b + 3)
                    pool.dma_start(d["new_h_sample"][g, b], new_h[b]).then_inc(hs_out[min(b, 1)], 16)
                    if b == 0:
                        save_a(1)
                wait(hs_out[0], 16 * (g + 1))
                wait(hs_out[1], 16 * (NB - 1) * (g + 1))
                wait(hp_out, 16 * (g + 1))
                wait(u_saved, 64 * (g + 1))
                pool.sem_inc(stored, 1)

            with pool.Fori(0, G) as g:
                group(g)
            pool.wait_ge(conva_ready[0], G + 1)
            pool.wait_ge(conva_ready[1], G + 1)
            pool.wait_ge(yb_ready, KM * (G - 1))
            for c in range(KM):
                pool.dma_start(x[:, c, :], x_spill[c]).then_inc(x_back, 16)
            pool.dma_start(d["new_b"], new_b[:]).then_inc(saved, 16)
            pool.wait_ge(saved, 16)

        @block.scalar
        def _(act):
            def split_hi(half, b, width=KM * P):
                act.wait_ge(raw_in[b], 16 * half + 16)
                act.wait_ge(job_done, 2 * half + b + 1)
                nc.scalar.copy(w_hi[:, b, 0:width], w_raw[:, b, 0:width]).then_inc(hi_done, 1)

            def job_ended(half, b):
                act.wait_ge(job_done, 2 * half + b + 3)

            def square(m, s, src):
                if not isinstance(m, int) or m >= 2:
                    act.wait_ge(acc_ready, m - 1)
                nc.scalar.activation(sq[:, s], src, ACT.Square).then_inc(sq_ready, 1)

            def inverse_root(e, i):
                act.wait_ge(var_ready, i + 1)
                nc.scalar.activation(rsq0, var, ACT.Ln).then_inc(ln_step, 1)
                act.wait_ge(ln_step, i + 1)
                nc.scalar.activation(rsq0, rsq0, ACT.Exp, scale=-0.5).then_inc(rsq_ready, 1)

            def xa_high(m, src, gain, c):
                nc.scalar.activation(xa_hi[:, c, :], src, ACT.Copy,
                                     scale=gains[:, gain, c:c + 1]).then_inc(xhi_ready, 1)

            def ffn(f, norm, updated):
                half, q0 = f * FFN2_HALF, NFF * f
                for p, n in enumerate(PARTS):
                    def gate_up(i, next_width=KM * P, first=False):
                        if not first or f:
                            split_hi(half + i, 1)
                        if first:
                            norm()
                        act.wait_ge(evac_done[0], half + i + 2)
                        nc.scalar.activation(silu_g[:], gate_s[:], ACT.Silu).then_inc(silu_ready, 1)
                        split_hi(half + i + 1, 0, next_width)
                        act.wait_ge(hid_ready, i + (q0 + 1))
                        nc.scalar.copy(h_hi[:, i, :], hid[:]).then_inc(hhi_ready, 1)

                    if p == 0:
                        gate_up(0, first=True)
                    with act.Fori(1 if p == 0 else 0, n - 1) as i:
                        gate_up(i)
                    gate_up(n - 1, n * P)
                    half += n
                    q0 += n

                    def down(j, next_width):
                        split_hi(half + j, 1, n * P)
                        if n < KM:
                            updated(2 * j)
                        if next_width:
                            split_hi(half + j + 1, 0, next_width)
                        if n < KM:
                            updated(2 * j + 1)

                    if n == KM:
                        with act.Fori(0, KM // 2 - 1) as j:
                            down(j, n * P)
                        down(KM // 2 - 1, KM * P)
                    else:
                        for j in range(KM // 2):
                            down(j, n * P if j < KM // 2 - 1 else (0 if f else KM * P))
                    half += KM // 2

            act.sem_inc(xbc_ready, 2)
            act.wait_ge(const_in, 16)
            split_hi(0, 0)
            for c in range(KM):
                act.wait_ge(x_in[c], 16)
                xa_high(S_FFN1 + c, x[:, c, :], 0, c)
                if c == 0:
                    split_hi(0, 1)
                square(c, c % 2, x[:, c, :])

            def norm_ffn1():
                inverse_root(N_FFN1, 0)

            def squares_for_mix(c):
                x_updated(act, MIX_HALF, c)
                square(Q_MIX + c, c % 2, x[:, c, :])

            ffn(0, norm_ffn1, squares_for_mix)
            split_hi(MIX_HALF, 1)
            act.wait_ge(wdt_in, 48)
            nc.scalar.copy(wdt_hi[:], wdt_raw[:]).then_inc(wdt_split, 1)
            inverse_root(N_MIX, 1)
            for c in range(KM):
                act.wait_ge(nin_ready, c + 1)
                xa_high(S_MIX + c, sq[:, c % 2], 1, c)
            act.wait_ge(cleared, 2)

            def dt_stage(k):
                if k == 1:
                    act.wait_ge(dt_dve, 1)
                    nc.scalar.activation(dts[:, 1], dts[:, 0], ACT.Abs).then_inc(dt_act, 1)
                    act.wait_ge(dt_act, 1)
                    nc.scalar.activation(dts[:, 1], dts[:, 1], ACT.Exp, scale=-1.0).then_inc(dt_act, 1)
                    nc.scalar.activation(dt_par[:, 2], dt_par[:, 1], ACT.Exp).then_inc(dt_act, 1)
                if k == 2:
                    act.wait_ge(dt_dve, 2)
                    nc.scalar.activation(dts[:, 3], dts[:, 2], ACT.Ln).then_inc(dt_act, 1)
                if k == 4:
                    act.wait_ge(cum_mm, 1)
                    nc.scalar.copy(cum_sb[0:H, 0:TP], pb[0:H, :]).then_inc(cum_copied, 1)
                    nc.scalar.copy(cum_sb[0:H, TP:T], pc[0:H, 0:P]).then_inc(cum_copied, 1)
                    nc.scalar.copy(tok[:, 1], pa[:, 0:NT * H].rearrange("p (t h) -> p t h", t=NT)
                                   ).then_inc(cum_copied, 1)
                if k == NX:
                    act.wait_ge(tok_done, 1)
                    nc.scalar.activation(tok[:, 2], tok[:, 2], ACT.Exp).then_inc(tok_done, 1)
                    act.wait_ge(tok_done, 2)

            def group(g, dt_stage=None):
                def at(k):
                    return MIX_HALF + g * (GJ // 2) + k // 2, k % 2

                def next_hi(k):
                    split_hi(*at(k + 1), KM * P if k + 1 < J_O or k + 1 == GJ else GC * P)

                def xbc_in(k):
                    s = k % 2
                    w = P_CB + k * (KB + 1) + KB - 1
                    job_ended(*at(k))
                    act.wait_ge(convb_ready, NX * g + k + 1)
                    act.wait_ge(xbc_ready, NX * g + k + 1)
                    smp, ps_smp = seqs(ext_b[:, s, EB:]), seqs(psj[:, s, 1, TP - TH:TH])
                    nc.scalar.activation(halved(conv_b[:, s]), job_out(s), ACT.Identity, bias=parg[:, w + 1:w + 2],
                                         scale=parg[:, w:w + 1]).then_inc(extb_ready, 1)
                    nc.scalar.copy(ext_b[:, s, HB:HB + TH], psj[:, s, 0, 0:TH]).then_inc(extb_ready, 1)
                    nc.scalar.copy(ext_b[:, s, HB + TH:EB], psj[:, s, 1, 0:TP - TH]).then_inc(extb_ready, 1)
                    nc.scalar.copy(smp[:, :, 0:HB], seqs(halo_b[:, g, k])).then_inc(extb_ready, 1)
                    nc.scalar.copy(new_b[:, g, k, 0:HB], psj[:, s, 1, TP - TH - HB:TP - TH]).then_inc(extb_ready, 1)
                    nc.scalar.copy(seqs(new_b[:, g, k, HB:]), ps_smp[:, :, TS - HB:]).then_inc(extb_ready, 1)
                    nc.scalar.copy(smp[:, :, HB:], ps_smp).then_inc(evac_done[s], 1)

                def skip(c):
                    act.wait_ge(xbc_ready, NX * g + c + 3)
                    nc.scalar.activation(y[:, c], xs[:, c], ACT.Copy,
                                         scale=parg[:, P_D + c:P_D + c + 1]).then_inc(dx_ready, 1)

                def xbc_silu(k):
                    act.wait_ge(tap_b, (2 * KB - 3) * (NX * g + k + 1))
                    act.wait_ge(convb_ready, NX * g + k + 3)
                    dst = xs[:, k, :] if k < GC else bc[:, k - GC, :]
                    nc.scalar.activation(dst, conv_b[:, k % 2], ACT.Silu).then_inc(xbc_ready, 1)

                def newest_tap(c):
                    w, w0 = (parg, P_CA) if c == 0 else (parc, 0)
                    act.wait_ge(u_part, 4 * g + 2 * c + 2)
                    act.wait_ge(evac_done[1], at((J_U0, J_U1)[c])[0] + 2)
                    if c == 1:
                        act.wait_ge(parc_ready, g + 1)
                    out = v[:, 2 * g + c]
                    for src, dst in ((ext_a[:, c, HA:EA], out[:, 0:TP]),
                                     (seqs(ext_a[:, c, EA:])[:, :, HA:], seqs(out[:, TP:T]))):
                        nc.scalar.activation(dst, src, ACT.Identity, bias=w[:, w0 + KA:w0 + KA + 1],
                                             scale=w[:, w0 + HA:w0 + HA + 1]).then_inc(newest_a[c], 1)

                def glu_gate(k):
                    job_ended(*at(k))
                    nc.scalar.activation(halved(sig[:]), job_out(k % 2), ACT.Sigmoid).then_inc(evac_done[k % 2], 1)

                def decay(t):
                    s, n = t % 2, NT * g + t
                    act.wait_ge(acb_in[t], 16 * g + 16)
                    if t < 2:
                        act.wait_ge(stored, g + 1)
                    else:
                        act.wait_ge(state_ready, LAST * g + t - 1)
                    ends = slice(P - 1, P) if t < LAST else slice(TS - 1, P, TS)
                    width = 1 if t < LAST else NB
                    nc.scalar.activation(el[:, s, :, 0:width], acb[:, s, :, ends], ACT.Exp).then_inc(dec_step, 1)
                    act.wait_ge(dec_step, (HG + 1) * n + 1)
                    for j in range(HG):
                        nc.scalar.activation(acb[:, s, j], acb[:, s, j], ACT.Relu, scale=-1.0,
                                             bias=tokg[:, 1, t, j:j + 1]).then_inc(dec_step, 1)
                    act.wait_ge(dec_step, (HG + 1) * (n + 1))
                    nc.scalar.activation(acb[:, s], acb[:, s], ACT.Exp, scale=-1.0).then_inc(dec_ready, 1)

                def decay_h(t):
                    act.wait_ge(ach_in[t], 32 * g + 32)
                    nc.scalar.activation(ach[:, t % 2], ach[:, t % 2], ACT.Exp).then_inc(dech_ready, 1)

                def xtl_out(t):
                    n = NT * g + t
                    act.wait_ge(xdt_ready, n + 1)
                    act.wait_ge(s_mm, LAST * g + t + 1)
                    for j in range(HG):
                        cols = slice(j * PD, (j + 1) * PD)
                        nc.scalar.activation(xtl[:, cols], xdt[:, cols], ACT.Copy,
                                             scale=tokg[:, 2, t, j:j + 1]).then_inc(xtl_ready, 1)

                def btok_out(t):
                    act.wait_ge(turned, NT * g + t + 1)
                    act.wait_ge(s_mm, LAST * g + t + 1)
                    act.wait_ge(cbm_ready, NT * g + t + 1)
                    nc.scalar.copy(btok[:], pb[:, 0:NS]).then_inc(btok_ready, 1)

                act.wait_ge(evac_done[1], MIX_HALF + g * (GJ // 2) + 1)
                act.wait_ge(conva_ready[0], g + 1)
                act.wait_ge(stored, g + 1)
                nc.scalar.copy(parg[:], par[:, g]).then_inc(parg_ready, 1)
                act.wait_ge(parg_ready, g + 1)
                for k in range(NX):
                    if k or not dt_stage:
                        next_hi(k)
                    if dt_stage:
                        dt_stage(k)
                    xbc_in(k)
                    if k >= 1:
                        xbc_silu(k - 1)
                    if k >= 3:
                        skip(k - 2)
                next_hi(J_U0)
                xbc_silu(NX - 1)
                if dt_stage:
                    dt_stage(NX)
                nc.scalar.copy(tokg[:].rearrange("p a t h -> p (a t) h"),
                               tok[:].rearrange("p a t h -> p (a t) h")[:, :, bass.ds(g * HG, HG)]
                               ).then_inc(tokg_ready, 1)
                act.wait_ge(tokg_ready, g + 1)
                if dt_stage:
                    act.wait_ge(cum_out, 16)
                skip(0)
                glu_gate(J_U0)
                next_hi(J_U0 + 1)
                decay(0)
                decay_h(0)
                btok_out(0)
                xtl_out(0)
                for c in range(GC):
                    k = J_Z + c
                    if c == 0:
                        act.wait_ge(s_mm, LAST * g + 2)
                        nc.scalar.copy(h_pr[:], pa).then_inc(state_ready, 1)
                    next_hi(k)
                    decay(c + 1)
                    if c == 0:
                        newest_tap(0)
                    btok_out(c + 1)
                    xtl_out(c + 1)
                    job_ended(*at(k))
                    nc.scalar.copy(halved(z[:, c]), job_out(k % 2)).then_inc(evac_done[k % 2], 1)
                    decay_h(c + 1)
                next_hi(J_U1)
                act.wait_ge(evac_done[1], at(J_U1)[0] + 1)
                for c in range(GC):
                    nc.scalar.activation(z[:, c], z[:, c], ACT.Silu).then_inc(z_ready, 1)
                for c in range(GC):
                    act.wait_ge(gz_ready, GC * g + c + 1)
                    nc.scalar.activation(gn_hi[:, c], y[:, c], ACT.Copy,
                                         scale=parg[:, P_N + c:P_N + c + 1]).then_inc(gnhi_ready, 1)
                act.wait_ge(hs_step, (NB - len(ON_SCALAR)) * g + 3)
                for c in range(GC):
                    square(Q_GROUP + GC * g + c, c % 2, y[:, c])
                glu_gate(J_U1)
                next_hi(J_U1 + 1)
                act.wait_ge(conva_ready[1], g + 1)
                nc.scalar.copy(parc[:], par[:, g, P_CA + KA + 1:P_D]).then_inc(parc_ready, 1)
                next_hi(J_O)
                inverse_root(N_GROUP + g, 2 + g)
                newest_tap(1)
                next_hi(J_O + 1)
                act.wait_ge(y_mm, NT * g + NT)
                for b in ON_SCALAR:
                    for j in range(HG):
                        cols = slice(j * PD, (j + 1) * PD)
                        nc.scalar.activation(new_h[b][:, cols], old_h[b][:, cols], ACT.Copy,
                                             scale=el[:, 0, j, b:b + 1]).then_inc(hs_scalar, 1)
                for k in range(J_O + 2, GJ):
                    next_hi(k)

            group(0, dt_stage)
            with act.Fori(1, G) as g:
                group(g)

            half = GATE_HALF

            act.wait_ge(yb_ready, KM * (G - 1))
            act.wait_ge(stored, G + 1)
            for c in range(KM):
                split_hi(half + (c + 1) // 2, (c + 1) % 2)
                job_ended(half + c // 2, c % 2)
                nc.scalar.activation(halved(gate_a[:, c]), job_out(c % 2), ACT.Sigmoid).then_inc(evac_done[c % 2], 1)
            half += KM // 2
            for c in range(KM):
                split_hi(half + (c + 1) // 2, (c + 1) % 2)
                if c == 1:
                    for i in range(KM):
                        act.wait_ge(vc_ready, i + 1)
                        square(Q_LN + i, i % 2, v[:, i])
                job_ended(half + c // 2, c % 2)
                if c >= 2:
                    act.wait_ge(gb_used, c - 1)
                nc.scalar.activation(halved(gate_b[:, c % 2]), job_out(c % 2), ACT.Sigmoid).then_inc(evac_done[c % 2], 1)
                if c == KM // 2 - 1:
                    inverse_root(N_LN, 6)
                if c in LN_CHUNKS:
                    for i in LN_CHUNKS[c]:
                        act.wait_ge(nin_ready, KM + i + 1)
                        nc.scalar.activation(v[:, i], v[:, i], ACT.Silu, bias=gains[:, 5, i:i + 1],
                                             scale=gains[:, 4, i:i + 1]).then_inc(vs_ready, 1)
            half += KM // 2
            split_hi(half, 1)
            for c in range(KM):
                act.wait_ge(vs_ready, c + 1)
                nc.scalar.copy(xa_hi[:, c], v[:, c]).then_inc(xhi_ready, 1)
            for c in range(KM):
                if c:
                    split_hi(half + (c + 1) // 2, (c + 1) % 2)
                act.wait_ge(merge_ready, c + 1)
                nc.scalar.copy(merged_hi[:, c], yb[:, c]).then_inc(mhi_ready, 1)
            half += KM // 2
            for c in range(KM):
                split_hi(half + (c + 1) // 2, (c + 1) % 2)
                x_updated(act, FFN2_HALF, c)
                square(Q_FFN2 + c, c % 2, x[:, c])
                xa_high(S_FFN2 + c, x[:, c], 2, c)

            def squares_for_output(c):
                x_updated(act, FFN2_HALF + FFN_HALVES, c)
                square(Q_OUT + c, c % 2, x[:, c, :])

            ffn(1, lambda: inverse_root(N_FFN2, 7), squares_for_output)
            inverse_root(N_OUT, 8)

        @block.vector
        def _(dve):
            def split_lo(half, b, width=KM * P):
                dve.wait_ge(hi_done, 2 * half + b + 1)
                nc.vector.tensor_tensor(w_lo[:, b, 0:width], w_raw[:, b, 0:width],
                                        w_hi[:, b, 0:width].bitcast(F32), ALU.subtract).then_inc(lo_done, 1)

            def job_ended(half, b):
                dve.wait_ge(job_done, 2 * half + b + 3)

            def accumulate(m, s, first):
                dve.wait_ge(sq_ready, m + 1)
                if first:
                    nc.vector.tensor_copy(acc[:], sq[:, s]).then_inc(acc_ready, 1)
                else:
                    dve.wait_ge(acc_ready, m)
                    nc.vector.tensor_tensor(acc[:], acc[:], sq[:, s], ALU.add).then_inc(acc_ready, 1)

            def variance(e, width, eps):
                dve.wait_ge(sum_ready, e + 1)
                nc.vector.tensor_scalar(halved(var), pab[:, :, 0:TH], 1.0 / width, eps,
                                        ALU.mult, ALU.add).then_inc(var_ready, 1)

            def newton(i):
                dve.wait_ge(rsq_ready, i + 1)
                nc.vector.scalar_tensor_tensor(rstd[:], var, -0.5, rsq0, ALU.mult, ALU.mult).then_inc(newton_step, 1)
                dve.wait_ge(newton_step, 2 * i + 1)
                nc.vector.tensor_tensor(rstd[:], rstd[:], rsq0, ALU.mult).then_inc(newton_step, 1)
                dve.wait_ge(newton_step, 2 * i + 2)
                nc.vector.scalar_tensor_tensor(rstd[:], rstd[:], 1.5, rsq0, ALU.add, ALU.mult).then_inc(rstd_ready, 1)
                dve.wait_ge(rstd_ready, i + 1)

            def xa_low(m, src, gain, c):
                dve.wait_ge(xhi_ready, m + 1)
                nc.vector.scalar_tensor_tensor(xa_lo[:, c], src, gains[:, gain, c:c + 1], xa_hi[:, c].bitcast(F32),
                                               ALU.mult, ALU.subtract).then_inc(xlo_ready, 1)

            def ffn(f, norm, updated):
                half, q0 = f * FFN2_HALF, NFF * f
                for p, n in enumerate(PARTS):
                    def gate_up(i, next_width=KM * P, first=False):
                        if not first or f:
                            split_lo(half + i, 1)
                        if first:
                            norm()
                        job_ended(half + i, 0)
                        nc.vector.tensor_tensor(halved(gate_s[:]), job_out(0), halved(rstd[:]),
                                                ALU.mult).then_inc(evac_done[0], 1)
                        split_lo(half + i + 1, 0, next_width)
                        job_ended(half + i, 1)
                        nc.vector.tensor_tensor(halved(up_s[:]), job_out(1), halved(rstd[:]),
                                                ALU.mult).then_inc(evac_done[1], 1)
                        dve.wait_ge(evac_done[1], half + i + 2)
                        dve.wait_ge(silu_ready, i + (q0 + 1))
                        nc.vector.tensor_tensor(hid[:], silu_g[:], up_s[:], ALU.mult).then_inc(hid_ready, 1)
                        dve.wait_ge(hhi_ready, i + (q0 + 1))
                        nc.vector.tensor_tensor(h_lo[:, i, :], hid[:], h_hi[:, i, :].bitcast(F32),
                                                ALU.subtract).then_inc(hlo_ready, 1)

                    if p == 0:
                        gate_up(0, first=True)
                    with dve.Fori(1 if p == 0 else 0, n - 1) as i:
                        gate_up(i)
                    gate_up(n - 1, n * P)
                    half += n
                    q0 += n

                    def down(j, next_width):
                        for b in range(2):
                            if b == 0:
                                split_lo(half + j, 1, n * P)
                            elif next_width:
                                split_lo(half + j + 1, 0, next_width)
                            job_ended(half + j, b)
                            xc = halved(x[:, j * 2 + b, :])
                            nc.vector.scalar_tensor_tensor(xc, job_out(b), 0.5, xc, ALU.mult,
                                                           ALU.add).then_inc(evac_done[b], 1)
                            if n < KM:
                                updated(2 * j + b)

                    if n == KM:
                        with dve.Fori(0, KM // 2 - 1) as j:
                            down(j, n * P)
                        down(KM // 2 - 1, KM * P)
                    else:
                        for j in range(KM // 2):
                            down(j, n * P if j < KM // 2 - 1 else (0 if f else KM * P))
                    half += KM // 2

            dve.sem_inc(evac_done[0], 1)
            dve.sem_inc(evac_done[1], 1)
            dve.sem_inc(lo_done, 2)
            dve.sem_inc(convb_ready, 2)
            dve.sem_inc(conva_ready[0], 1)
            dve.sem_inc(conva_ready[1], 1)
            dve.sem_inc(y_done, 1)
            dve.sem_inc(hs_new, 2)
            split_lo(0, 0)
            for c in range(KM):
                dve.wait_ge(x_in[c], 16)
                xa_low(S_FFN1 + c, x[:, c], 0, c)
                if c == 0:
                    split_lo(0, 1)
                accumulate(Q_FFN1 + c, c % 2, c == 0)

            def norm_ffn1():
                variance(N_FFN1, DM, RMS_EPS)
                newton(0)

            ffn(0, norm_ffn1, lambda c: accumulate(Q_MIX + c, c % 2, c == 0))
            split_lo(MIX_HALF, 1)
            dve.wait_ge(wdt_split, 1)
            nc.vector.tensor_tensor(wdt_lo[:], wdt_raw[:], wdt_hi[:].bitcast(F32), ALU.subtract).then_inc(wdt_lo_ready, 1)
            variance(N_MIX, DM, RMS_EPS)
            newton(1)
            for c in range(KM + 1):
                if c < KM:
                    if c >= 2:
                        dve.wait_ge(xlo_ready, S_MIX + c - 1)
                    nc.vector.tensor_tensor(sq[:, c % 2], x[:, c], rstd[:], ALU.mult).then_inc(nin_ready, 1)
                if c:
                    dve.wait_ge(nin_ready, c)
                    xa_low(S_MIX + c - 1, sq[:, (c - 1) % 2], 1, c - 1)
            dve.wait_ge(spilled, 16 * KM)
            nc.vector.memset(ext_a[:, :, 0:HA], 0.0).then_inc(cleared, 1)
            nc.vector.memset(ext_b[:, :, 0:HB], 0.0).then_inc(cleared, 1)

            def by_tile(ap):
                return ap.rearrange("p (t h) -> p t h", t=NT)

            def dt_stage(k):
                if k == 1:
                    dve.wait_ge(dt_mm, 1)
                    nc.vector.tensor_tensor(by_tile(dts[:, 0]), by_tile(pc[:, 0:NT * H]),
                                            dt_par[:, 0].unsqueeze(1).broadcast_to([P, NT, H]),
                                            ALU.add).then_inc(dt_dve, 1)
                if k == 2:
                    dve.wait_ge(dt_act, 2)
                    nc.vector.tensor_scalar(dts[:, 2], dts[:, 1], 1.0, None, ALU.add).then_inc(dt_dve, 1)
                    dve.wait_ge(dt_dve, 2)
                    nc.vector.scalar_tensor_tensor(dts[:, 4], dts[:, 2], 1.0, dts[:, 1], ALU.subtract,
                                                   ALU.subtract).then_inc(dt_dve, 1)
                    nc.vector.reciprocal(dts[:, 5], dts[:, 2]).then_inc(dt_dve, 1)
                    dve.wait_ge(dt_dve, 4)
                    nc.vector.tensor_tensor(dts[:, 4], dts[:, 4], dts[:, 5], ALU.mult).then_inc(dt_dve, 1)
                if k == 3:
                    dve.wait_ge(dt_dve, 5)
                    dve.wait_ge(dt_act, 4)
                    nc.vector.tensor_tensor(dts[:, 3], dts[:, 3], dts[:, 4], ALU.subtract).then_inc(dt_dve, 1)
                    dve.wait_ge(dt_dve, 6)
                    nc.vector.scalar_tensor_tensor(tok[:, 0].rearrange("p t h -> p (t h)"), dts[:, 0], 0.0,
                                                   dts[:, 3], ALU.max, ALU.add).then_inc(dt_dve, 1)
                    dve.wait_ge(dt_dve, 7)
                    nc.vector.scalar_tensor_tensor(by_tile(dts[:, 1]), tok[:, 0], -1.0,
                                                   dt_par[:, 2].unsqueeze(1).broadcast_to([P, NT, H]),
                                                   ALU.mult, ALU.mult).then_inc(dt_dve, 1)
                if k == 5:
                    dve.wait_ge(cum_copied, 3)
                    nc.vector.tensor_tensor(tok[:, 2], by_tile(pa[:, 256:256 + NT * H]), tok[:, 1],
                                            ALU.subtract).then_inc(tok_done, 1)

            def conv_glu(k, c, g):
                if not TAPS[c].get(k):
                    return
                base = (2 * KA - 3) * g
                start = sum(taps for place, taps in TAPS[c].items() if place < k)
                w, w0 = (parg, P_CA) if c == 0 else (parc, 0)
                out = v[:, 2 * g + c]
                if start == 0:
                    dve.wait_ge(newest_a[c], 2 * g + 2)
                for j in range(start, start + TAPS[c][k]):
                    for s, (src, dst) in enumerate(((ext_a[:, c, j:j + TP], out[:, 0:TP]),
                                                    (seqs(ext_a[:, c, EA:])[:, :, j:j + TS], seqs(out[:, TP:T])))):
                        if j:
                            dve.wait_ge(tap_a[c], base + 2 * j - 1 + s)
                        nc.vector.scalar_tensor_tensor(dst, src, w[:, w0 + j:w0 + j + 1], dst, ALU.mult, ALU.add
                                                       ).then_inc(conva_ready[c] if s and j == KA - 2 else tap_a[c], 1)

            def group(g, carried=True):
                def at(k):
                    return MIX_HALF + g * (GJ // 2) + k // 2, k % 2

                def evacuated(k):
                    half, b = at(k)
                    dve.wait_ge(evac_done[b], half + 2)

                def param(column):
                    return parg[:, column:column + 1]

                def conv_xbc(k):
                    s, m, taps = k % 2, NX * g + k, KB - 1
                    dve.wait_ge(extb_ready, 6 * m + 6)
                    evacuated(k)
                    w0 = P_CB + k * (KB + 1)
                    for j in range(taps):
                        if j:
                            dve.wait_ge(tap_b, (2 * taps - 1) * m + 2 * j - 1)
                        nc.vector.scalar_tensor_tensor(conv_b[:, s, 0:TP], ext_b[:, s, j:j + TP], param(w0 + j),
                                                       conv_b[:, s, 0:TP], ALU.mult, ALU.add).then_inc(tap_b, 1)
                        if j:
                            dve.wait_ge(tap_b, (2 * taps - 1) * m + 2 * j)
                        smp = seqs(conv_b[:, s, TP:])
                        nc.vector.scalar_tensor_tensor(smp, seqs(ext_b[:, s, EB:])[:, :, j:j + TS], param(w0 + j), smp,
                                                       ALU.mult, ALU.add).then_inc(tap_b if j < taps - 1 else convb_ready, 1)

                def glu(k, c):
                    evacuated(k - 1)
                    dve.wait_ge(conva_ready[c], g + 1)
                    dve.wait_ge(halo_a_in[c], 16 * (g + 1))
                    job_ended(*at(k))
                    b = k % 2
                    nc.vector.tensor_tensor(ext_a[:, c, HA:HA + TH], psj[:, b, 0, 0:TH], sig[:, 0:TH],
                                            ALU.mult).then_inc(u_part, 1)
                    nc.vector.tensor_tensor(ext_a[:, c, HA + TH:EA], psj[:, b, 1, 0:TP - TH], sig[:, TH:TP],
                                            ALU.mult).then_inc(u_part, 1)
                    nc.vector.tensor_tensor(seqs(ext_a[:, c, EA:])[:, :, HA:], seqs(psj[:, b, 1, TP - TH:TH]),
                                            seqs(sig[:, TP:T]), ALU.mult).then_inc(evac_done[b], 1)

                def heads(ap):
                    return ap.rearrange("p (h q) -> p h q", h=HG)

                def over_width(ap, width):
                    return ap.unsqueeze(2).broadcast_to([P, ap.shape[1], width])

                def over_heads(ap):
                    return ap.unsqueeze(1).broadcast_to([P, HG, ap.shape[1]])

                def state(t):
                    dve.wait_ge(s_mm, LAST * g + t + 2)
                    dve.wait_ge(state_ready, LAST * g + t)
                    nc.vector.tensor_tensor(heads(h_pr[:]), heads(h_pr[:]), over_width(el[:, t % 2, :, 0], PD),
                                            ALU.mult).then_inc(state_step, 1)
                    dve.wait_ge(state_step, (LAST - 1) * g + t)
                    nc.vector.tensor_tensor(h_pr[:], h_pr[:], pa, ALU.add).then_inc(state_ready, 1)

                def prepare(t):
                    n = NT * g + t
                    dve.wait_ge(turned, n + 1)
                    nc.vector.tensor_tensor(heads(xdt[:]), heads(pa), over_width(tokg[:, 0, t], PD),
                                            ALU.mult).then_inc(xdt_ready, 1)
                    nc.vector.tensor_tensor(cbm[:], pb[:, NS:NS + P], const[:, TRI if t < LAST else TRI_S],
                                            ALU.mult).then_inc(cbm_ready, 1)
                    dve.wait_ge(dec_ready, n + 1)
                    dve.wait_ge(cbm_ready, n + 1)
                    nc.vector.tensor_tensor(mdec[:], acb[:, t % 2], over_heads(cbm[:]), ALU.mult).then_inc(m_ready, 1)

                def y_out(t):
                    yt, at_tile = y[:, :, t * P:(t + 1) * P], ach[:, t % 2]
                    pcv, pdv = (ap[:].rearrange("p (c i) -> p c i", c=GC) for ap in (pc, pd))
                    if t == 0:
                        dve.wait_ge(dx_ready, GC * (g + 1))
                    dve.wait_ge(y_mm, NT * g + t + 1)
                    if t == 0:
                        nc.vector.tensor_tensor(yt, yt, pcv, ALU.add).then_inc(y_done, 1)
                        return
                    nc.vector.tensor_tensor(yt, yt, pcv, ALU.add).then_inc(y_step, 1)
                    dve.wait_ge(dech_ready, NT * g + t + 1)
                    nc.vector.tensor_tensor(at_tile, pdv, at_tile, ALU.mult).then_inc(y_step, 1)
                    dve.wait_ge(y_step, 2 * LAST * g + 2 * t)
                    nc.vector.tensor_tensor(yt, yt, at_tile, ALU.add).then_inc(y_done, 1)

                def b_alone():
                    dve.wait_ge(btok_ready, NT * g + NT)
                    dve.wait_ge(y_done, NT * g + LAST + 1)
                    for dst, s in ((ach[:, 1], slice(0, NB // 2)), (acb[:, 1, NB // 2:], slice(NB // 2, NB))):
                        nc.vector.tensor_tensor(dst, btok[:].unsqueeze(1).broadcast_to([P, NB // 2, NS]),
                                                over_width(bmask[:, s], NS), ALU.mult).then_inc(bm_ready, 1)

                def decayed(b):
                    nc.vector.tensor_tensor(heads(new_h[b]), heads(old_h[b]), over_width(el[:, 0, :, b], PD),
                                            ALU.mult).then_inc(hs_step, 1)

                def sample_state(b):
                    m = NB * g + b
                    dve.wait_ge(hs_step, (NB - len(ON_SCALAR)) * (g + 1))
                    if b in ON_SCALAR:
                        dve.wait_ge(hs_scalar, len(ON_SCALAR) * HG * (g + 1))
                    dve.wait_ge(hs_mm, m + 1)
                    nc.vector.tensor_tensor(new_h[b], new_h[b], (pc, pd)[b % 2][:], ALU.add).then_inc(hs_new, 1)

                dve.wait_ge(parg_ready, g + 1)
                for k in range(GJ):
                    if k or carried:
                        split_lo(*at(k + 1), KM * P if k + 1 < J_O or k + 1 == GJ else GC * P)
                    if carried:
                        conv_glu(GJ + k, 1, g - 1)
                    else:
                        dt_stage(k)
                    if k < NX:
                        conv_xbc(k)
                    if k == J_U0 + 1:
                        dve.wait_ge(tokg_ready, g + 1)
                        prepare(0)
                        glu(k, 0)
                        if carried:
                            conv_glu(GJ + k + .5, 1, g - 1)
                    if J_Z <= k < J_U1:
                        t = k - J_Z + 1
                        if t > 1:
                            state(t - 1)
                        y_out(t - 1)
                        prepare(t)
                        if t == LAST:
                            b_alone()
                        conv_glu(k + .5, 0, g)
                    if k == J_U1:
                        conv_glu(k, 0, g)
                        y_out(LAST)
                        dve.wait_ge(y_done, NT * g + NT + 1)
                        for c in range(GC):
                            dve.wait_ge(z_ready, GC * g + c + 1)
                            nc.vector.tensor_tensor(y[:, c], y[:, c], z[:, c], ALU.mult).then_inc(gz_ready, 1)
                        dve.wait_ge(gz_ready, GC * g + GC)
                        for b in (1, 2, 3):
                            decayed(b)
                        for c in range(GC):
                            dve.wait_ge(gnhi_ready, GC * g + c + 1)
                            nc.vector.scalar_tensor_tensor(gn_lo[:, c], y[:, c], param(P_N + c),
                                                           gn_hi[:, c].bitcast(F32), ALU.mult,
                                                           ALU.subtract).then_inc(gnlo_ready, 1)
                            accumulate(Q_GROUP + GC * g + c, c % 2, c == 0)
                        for b in (0, 4, 5):
                            decayed(b)
                    if k == J_U1 + 1:
                        dve.wait_ge(hs_step, (NB - len(ON_SCALAR)) * (g + 1))
                        variance(N_GROUP + g, GC * P, RMS_EPS)
                        sample_state(0)
                        glu(k, 1)
                        sample_state(1)
                        conv_glu(k + .5, 0, g)
                    if k >= J_O:
                        half, b = at(k)
                        c = k - J_O
                        if c == 0:
                            dve.wait_ge(hs_out[0], 16 * (g + 1))
                            newton(2 + g)
                        job_ended(half, b)
                        if carried:
                            nc.vector.tensor_tensor(halved(y[:, c % 2]), job_out(b), halved(rstd[:]),
                                                    ALU.mult).then_inc(evac_done[b], 1)
                            evacuated(k)
                            nc.vector.tensor_tensor(yb[:, c], yb[:, c], y[:, c % 2], ALU.add).then_inc(yb_ready, 1)
                        else:
                            nc.vector.tensor_tensor(halved(yb[:, c]), job_out(b), halved(rstd[:]),
                                                    ALU.mult).then_inc(evac_done[b], 1)
                        if c < NB - 2:
                            sample_state(c + 2)
                        conv_glu(k, 0, g)
                        conv_glu(k, 1, g)

            group(0, carried=False)
            with dve.Fori(1, G) as g:
                group(g)

            half = GATE_HALF
            for c in range(KM):
                split_lo(half + (c + 1) // 2, (c + 1) % 2)
                conv_glu(GJ + c, 1, G - 1)
                conv_glu(GJ + c + .5, 1, G - 1)
                if c == 3:
                    dve.wait_ge(conva_ready[0], G + 1)
                    dve.wait_ge(conva_ready[1], G)
                    nc.vector.tensor_tensor(acc[:], v[:, 0], v[:, 1], ALU.add).then_inc(vsum_step, 1)
                    for i in range(2, KM - 1):
                        dve.wait_ge(vsum_step, i - 1)
                        nc.vector.tensor_tensor(acc[:], acc[:], v[:, i], ALU.add).then_inc(vsum_step, 1)
            dve.wait_ge(tap_a[1], (2 * KA - 3) * G)
            dve.wait_ge(conva_ready[1], G + 1)
            dve.wait_ge(vsum_step, KM - 2)
            nc.vector.tensor_tensor(acc[:], acc[:], v[:, KM - 1], ALU.add).then_inc(vsum_step, 1)
            half += KM // 2
            dve.wait_ge(yb_ready, KM * (G - 1))
            for c in range(KM):
                split_lo(half + (c + 1) // 2, (c + 1) % 2)
                if c == 0:
                    dve.wait_ge(sum_ready, N_MEAN + 1)
                    nc.vector.tensor_scalar(halved(var), pab[:, :, 0:TH], 1.0 / DM, None, ALU.mult).then_inc(vsum_step, 1)
                    dve.wait_ge(vsum_step, KM)
                    for i in range(KM):
                        nc.vector.tensor_tensor(v[:, i], v[:, i], var, ALU.subtract).then_inc(vc_ready, 1)
                if c == 1:
                    for i in range(KM):
                        accumulate(Q_LN + i, i % 2, i == 0)
                if c == KM // 2 - 1:
                    variance(N_LN, DM, LN_EPS)
                if c >= KM // 2:
                    if c == KM // 2:
                        newton(6)
                    for i in LN_CHUNKS.get(c, ()):
                        nc.vector.tensor_tensor(v[:, i], v[:, i], rstd[:], ALU.mult).then_inc(nin_ready, 1)
                dve.wait_ge(evac_done[c % 2], half + c // 2 + 2)
                nc.vector.tensor_tensor(yb[:, c], yb[:, c], gate_b[:, c % 2], ALU.mult).then_inc(gb_used, 1)
            half += KM // 2
            split_lo(half, 1)
            for c in range(KM):
                dve.wait_ge(xhi_ready, S_LN + c + 1)
                nc.vector.tensor_tensor(xa_lo[:, c], v[:, c], xa_hi[:, c].bitcast(F32), ALU.subtract).then_inc(xlo_ready, 1)
            dve.wait_ge(gb_used, KM)
            for c in range(KM):
                b = c % 2
                if c:
                    split_lo(half + (c + 1) // 2, (c + 1) % 2)
                job_ended(half + c // 2, b)
                nc.vector.tensor_tensor(halved(prod[:]), job_out(b), halved(gate_a[:, c]), ALU.mult).then_inc(evac_done[b], 1)
                dve.wait_ge(evac_done[b], half + c // 2 + 2)
                nc.vector.tensor_tensor(yb[:, c], yb[:, c], prod[:], ALU.add).then_inc(merge_ready, 1)
                dve.wait_ge(mhi_ready, c + 1)
                nc.vector.tensor_tensor(merged_lo[:, c], yb[:, c], merged_hi[:, c].bitcast(F32),
                                        ALU.subtract).then_inc(mlo_ready, 1)
            half += KM // 2
            dve.wait_ge(x_back, 16 * KM)
            for c in range(KM):
                b = c % 2
                split_lo(half + (c + 1) // 2, (c + 1) % 2)
                job_ended(half + c // 2, b)
                nc.vector.tensor_tensor(halved(x[:, c]), job_out(b), halved(x[:, c]), ALU.add).then_inc(evac_done[b], 1)
                accumulate(Q_FFN2 + c, b, c == 0)
                xa_low(S_FFN2 + c, x[:, c], 2, c)

            def norm_ffn2():
                variance(N_FFN2, DM, RMS_EPS)
                newton(7)

            ffn(1, norm_ffn2, lambda c: accumulate(Q_OUT + c, c % 2, c == 0))
            variance(N_OUT, DM, RMS_EPS)
            newton(8)
            for c in range(KM):
                nc.vector.scalar_tensor_tensor(x[:, c], x[:, c], gains[:, 3, c:c + 1], rstd[:], ALU.mult,
                                               ALU.mult).then_inc(out_ready, 1)

        @block.tensor
        def _(pe):
            def job(half, b, chunks, in_hi, in_lo, before=None):
                pe.wait_ge(lo_done, 2 * half + b + 3)
                pe.wait_ge(evac_done[b], half + 1)
                for k in range(chunks):
                    if before:
                        before(k)
                    cols = slice(k * P, (k + 1) * P)
                    for n, (w, act_in) in enumerate(((w_hi, in_hi), (w_hi, in_lo), (w_lo, in_hi))):
                        for u in range(2):
                            last = nc.tensor.matmul(psj[:, b, u, 0:TH], w[:, b, cols],
                                                    act_in[:, k, u * TH:(u + 1) * TH],
                                                    start=(k == 0 and n == 0), stop=(k == chunks - 1 and n == 2))
                last.then_inc(job_done, 1)

            def pair_of_jobs(half, chunks, in_hi, in_lo, before):
                for k in range(chunks):
                    before(k)
                    cols = slice(k * P, (k + 1) * P)
                    for b in range(2):
                        if k == 0:
                            pe.wait_ge(lo_done, 2 * half + b + 3)
                            pe.wait_ge(evac_done[b], half + 1)
                        for n, (w, act_in) in enumerate(((w_hi, in_hi), (w_hi, in_lo), (w_lo, in_hi))):
                            for u in range(2):
                                last = nc.tensor.matmul(psj[:, b, u, 0:TH], w[:, b, cols],
                                                        act_in[:, k, u * TH:(u + 1) * TH],
                                                        start=(k == 0 and n == 0), stop=(k == chunks - 1 and n == 2))
                        if k == chunks - 1:
                            last.then_inc(job_done, 1)

            def token_sums():
                for u in range(2):
                    last = nc.tensor.matmul(pab[:, u, 0:TH], const[:, ONES], acc[:, u * TH:(u + 1) * TH],
                                            start=True, stop=True)
                last.then_inc(sum_ready, 1)

            def ffn(f):
                half, q0 = f * FFN2_HALF, NFF * f

                def first_input(k):
                    m = (S_FFN1, S_FFN2)[f] + k
                    pe.wait_ge(xlo_ready, m + 1)

                def norm_sum(k):
                    if k == 1:
                        pe.wait_ge(par_in, 64)
                        pe.wait_ge(acc_ready, (Q_FFN1, Q_FFN2)[f] + KM)
                        token_sums()

                for p, n in enumerate(PARTS):
                    if p == 0:
                        if f == 0:
                            def input_and_sum(k):
                                first_input(k)
                                if k == KM - 1:
                                    norm_sum(1)
                            pair_of_jobs(half, KM, xa_hi, xa_lo, input_and_sum)
                        else:
                            job(half, 0, KM, xa_hi, xa_lo, first_input)
                            job(half, 1, KM, xa_hi, xa_lo, norm_sum)
                    with pe.Fori(1 if p == 0 else 0, n) as i:
                        for b in range(2):
                            job(half + i, b, KM, xa_hi, xa_lo)
                    half += n

                    def hidden(k, q0=q0):
                        pe.wait_ge(hlo_ready, q0 + k + 1)

                    job(half, 0, n, h_hi, h_lo, hidden)
                    job(half, 1, n, h_hi, h_lo)
                    with pe.Fori(1, KM // 2) as j:
                        for b in range(2):
                            job(half + j, b, n, h_hi, h_lo)
                    half += KM // 2
                    q0 += n

            pe.sem_inc(job_done, 2)
            pe.sem_inc(s_mm, 1)
            ffn(0)
            pe.wait_ge(acc_ready, Q_MIX + KM)
            token_sums()

            def dt_products():
                pe.wait_ge(wdt_lo_ready, 1)
                for t in range(NT):
                    tokens = slice(t * P, (t + 1) * P)
                    for k in range(KM):
                        cols = slice(k * H, (k + 1) * H)
                        for n, (a, w) in enumerate(((xa_hi, wdt_hi), (xa_lo, wdt_hi), (xa_hi, wdt_lo))):
                            last = nc.tensor.matmul(pc[:, t * H:(t + 1) * H], a[:, k, tokens], w[:, cols],
                                                    start=(k == 0 and n == 0), stop=(k == KM - 1 and n == 2))
                last.then_inc(dt_mm, 1)

            def cumulate():
                pe.wait_ge(dt_dve, 8)
                for t in range(NT):
                    tri, ones = (TRI, ONES) if t < LAST else (TRI_S, BLK_S)
                    da = dts[:, 1, t * H:(t + 1) * H]
                    nc.tensor.matmul(pa[:, t * H:(t + 1) * H], const[:, tri], da, start=True, stop=True)
                    nc.tensor.matmul(pa[:, 256 + t * H:256 + (t + 1) * H], const[:, ones], da, start=True, stop=True)
                    out = pb[0:H, t * P:(t + 1) * P] if t < LAST else pc[0:H, 0:P]
                    last = nc.tensor.matmul(out, da, const[:, tri], start=True, stop=True)
                last.then_inc(cum_mm, 1)

            def group(g, first=False):
                def run(k, before=None):
                    half, b = MIX_HALF + g * (GJ // 2) + k // 2, k % 2
                    if k < J_O:
                        job(half, b, KM, xa_hi, xa_lo, before)
                    else:
                        job(half, b, GC, gn_hi, gn_lo, before)

                def turn(t):
                    cols = slice(t * P, (t + 1) * P)
                    if t == 0:
                        pe.wait_ge(tokg_ready, g + 1)
                        pe.wait_ge(xbc_ready, NX * g + NX + 2)
                        pe.wait_ge(var_ready, g + 2)
                    else:
                        pe.wait_ge(state_ready, LAST * g + t)
                    for c in range(GC):
                        nc.tensor.transpose(pa[:, c * P:(c + 1) * P], xs[:, c, cols], const[:, IDENT])
                    nc.tensor.transpose(pb[:, 0:P], bc[:, 0, cols], const[:, IDENT])
                    nc.tensor.matmul(pb[:, P:2 * P], bc[:, 0, cols], bc[:, 1, cols], start=True,
                                     stop=True).then_inc(turned, 1)

                def tile(t):
                    n = NT * g + t
                    cols = slice(t * P, (t + 1) * P)
                    pe.wait_ge(xdt_ready, n + 1)
                    pe.wait_ge(m_ready, n + 1)
                    pe.wait_ge(y_done, n + 1)
                    for c in range(GC):
                        for e in range(2):
                            hh = 2 * c + e
                            last = nc.tensor.matmul(pc[e * PD:(e + 1) * PD, c * P:(c + 1) * P],
                                                    xdt[:, hh * PD:(hh + 1) * PD], mdec[:, hh], start=True, stop=True)
                    if t == 0:
                        last.then_inc(y_mm, 1)
                    elif t < LAST:
                        pe.wait_ge(state_ready, LAST * g + t)
                        for c in range(GC):
                            last = nc.tensor.matmul(pd[:, c * P:(c + 1) * P], h_pr[:, c * P:(c + 1) * P],
                                                    bc[:, 1, cols], start=True, stop=True)
                        last.then_inc(y_mm, 1)
                    if t < LAST:
                        pe.wait_ge(btok_ready, n + 1)
                        pe.wait_ge(xtl_ready, HG * (n + 1))
                        nc.tensor.matmul(pa, btok[:], xtl[:], start=True, stop=True).then_inc(s_mm, 1)
                        return
                    pe.wait_ge(hs_in, 16 * NB * (g + 1))
                    for b in range(NB):
                        for c in range(GC):
                            out = pd[:, c * P + b * TS:c * P + (b + 1) * TS]
                            last = nc.tensor.matmul(out, old_h[b][:, c * P:(c + 1) * P],
                                                    bc[:, 1, TP + b * TS:TP + (b + 1) * TS], start=True, stop=True)
                    last.then_inc(y_mm, 1)

                def sample(b):
                    if b == 0:
                        pe.wait_ge(bm_ready, 2 * g + 2)
                        pe.wait_ge(xtl_ready, HG * NT * (g + 1))
                        pe.wait_ge(y_done, NT * g + NT + 1)
                    pe.wait_ge(hs_new, NB * g + b + 1)
                    nc.tensor.matmul((pc, pd)[b % 2][:], b_one[b], xtl[:], start=True, stop=True).then_inc(hs_mm, 1)

                for k in range(GJ):
                    t = k - (J_U0 + 1)
                    if 0 <= t < NT:
                        if t == 0:
                            pe.wait_ge(hs_new, NB * g + 2)
                        run(k, lambda i, t=t: turn(t) if i == KM // 2 else None)
                        tile(t)
                    elif k == J_U1 + 1:
                        def between(i):
                            if i in (0, 3):
                                sample(i // 3)
                            if i == KM - 1:
                                pe.wait_ge(acc_ready, Q_GROUP + GC * (g + 1))
                                token_sums()
                        run(k, between)
                    elif k >= J_O:
                        run(k, (lambda i: pe.wait_ge(gnlo_ready, GC * g + i + 1)) if k == J_O else None)
                        if k - J_O < NB - 2:
                            sample(k - J_O + 2)
                    elif k == 0 and first:
                        pair_of_jobs(MIX_HALF, KM, xa_hi, xa_lo, lambda i: pe.wait_ge(xlo_ready, S_MIX + i + 1))
                        dt_products()
                    elif k == 1 and first:
                        pass
                    else:
                        if k == 4 and first:
                            cumulate()
                        run(k)

            group(0, first=True)
            with pe.Fori(1, G) as g:
                group(g)

            half = GATE_HALF
            with pe.Fori(0, KM // 2) as j:
                for b in range(2):
                    job(half + j, b, KM, xa_hi, xa_lo)
            half += KM // 2

            def mean_sum(k):
                if k == KM // 2:
                    pe.wait_ge(vsum_step, KM - 1)
                    token_sums()

            for c in range(KM):
                job(half + c // 2, c % 2, KM, xa_hi, xa_lo, mean_sum if c == 0 else None)
                if c == 2:
                    pe.wait_ge(acc_ready, Q_LN + KM)
                    token_sums()
            half += KM // 2
            pair_of_jobs(half, KM, xa_hi, xa_lo, lambda k: pe.wait_ge(xlo_ready, S_LN + k + 1))
            with pe.Fori(1, KM // 2) as j:
                for b in range(2):
                    job(half + j, b, KM, xa_hi, xa_lo)
            half += KM // 2
            job(half, 0, KM, merged_hi, merged_lo, lambda k: pe.wait_ge(mlo_ready, k + 1))
            job(half, 1, KM, merged_hi, merged_lo)
            with pe.Fori(1, KM // 2) as j:
                for b in range(2):
                    job(half + j, b, KM, merged_hi, merged_lo)
            ffn(1)
            pe.wait_ge(acc_ready, Q_OUT + KM)
            token_sums()


NAMES = ("x", "w_gu", "w_down", "w_down_last", "w_mix", "w_ssm", "w_tail", "w_dt", "gains", "par", "halo_a", "halo_b",
         "dt_bias", "a_log", "h_sample", "const", "bmask")
OUTS = {"y": (KM, P, T), "new_a_prompt": (KM, P, HA), "new_a_sample": (KM, P, NB, HA),
        "new_b": (P, G, NX, HB + NB * HB), "new_h_prompt": (G, NS, HG * PD), "new_h_sample": (G, NB, NS, HG * PD)}


def lay_out(inp):
    import numpy as np

    a = {k: np.asarray(v) for k, v in inp.items()}

    def blocks(w):
        k, n = w.shape
        return np.ascontiguousarray(w.reshape(k // P, P, n // P, P).transpose(2, 1, 0, 3)).reshape(n // P, P, k)

    def columns(vec):
        return vec.reshape(-1, P).T

    out = {}
    xt = np.concatenate([a["x_prompt"].reshape(TP, DM), a["x_sample"].reshape(NB * TS, DM)], 0).T
    out["x"] = xt.reshape(KM, P, T)
    w_gu, w_down, w_last = [], [], []
    for f in ("ffn1", "ffn2"):
        w_gu.append(np.stack([blocks(a[f + "_w_gate"][0]), blocks(a[f + "_w_up"][0])], 1))
        down = a[f + "_w_down"][0]
        w_down.append(np.stack([blocks(down[p * DM:(p + 1) * DM]) for p in range(2)], 0))
        w_last.append(blocks(down[2 * DM:]))
    out["w_gu"] = np.stack(w_gu)
    out["w_down"] = np.stack(w_down).reshape(2, 2, KM // 2, 2, P, DM)
    out["w_down_last"] = np.stack(w_last).reshape(2, KM // 2, 2, P, PARTS[2] * P)
    w_in = a["w_in"][0]
    o_z, o_x = 2 * DM, 2 * DM + G * GC * P
    o_dt = o_x + G * NX * P
    o_g = o_dt + H
    wb = blocks(np.concatenate([w_in[:, :o_dt], w_in[:, o_g:]], 1))
    u0, z0, x0, g0 = 0, o_z // P, o_x // P, o_dt // P
    order = []
    for g in range(G):
        xbc = [x0 + g * GC + c for c in range(GC)] + [x0 + G * GC + g, x0 + G * GC + G + g]
        glu = [[KM + 2 * g + c, u0 + 2 * g + c] for c in range(2)]
        order.append(xbc + glu[0] + [z0 + g * GC + c for c in range(GC)] + glu[1])
    out["w_mix"] = wb[np.array(order)]
    out["w_ssm"] = np.stack([blocks(a["w_ssm_out"][0][g * GC * P:(g + 1) * GC * P]) for g in range(G)])
    out["w_tail"] = np.concatenate([wb[g0:g0 + 2 * KM], blocks(a["w_conv_a_out"][0]), blocks(a["w_out"][0])]
                                   ).reshape(2 * KM, 2, P, DM)
    out["w_dt"] = w_in[:, o_dt:o_g].reshape(KM, P, H).transpose(1, 0, 2).reshape(P, KM * H)
    out["gains"] = np.stack([columns(a[n].reshape(-1)) for n in
                             ("norm_ffn1", "norm_mix", "norm_ffn2", "norm_final", "ln_conv_g", "ln_conv_b")], 1)
    par = np.zeros((P, G, NPAR), np.float32)
    cb = np.concatenate([a["conv_b_w"][0], a["conv_b_b"]], 0).reshape(KB + 1, -1, P)
    ca = np.concatenate([a["conv_a_w"][0], a["conv_a_b"]], 0).reshape(KA + 1, -1, P)
    head_d = columns(np.repeat(a["d_skip"][0], PD))
    ng = columns(a["ssm_norm_g"][0])
    sb_ = a["state_conv_b"][0].reshape(NB, HB, -1, P)
    halo_b = np.zeros((P, G, NX, NB * HB), np.float32)
    for g in range(G):
        for k in range(NX):
            ch = g * GC + k if k < GC else G * GC + (k - GC) * G + g
            par[:, g, P_CB + k * (KB + 1):P_CB + (k + 1) * (KB + 1)] = cb[:, ch].T
            halo_b[:, g, k] = sb_[:, :, ch].transpose(2, 0, 1).reshape(P, NB * HB)
        for c in range(2):
            par[:, g, P_CA + c * (KA + 1):P_CA + (c + 1) * (KA + 1)] = ca[:, 2 * g + c].T
        par[:, g, P_D:P_D + GC] = head_d[:, g * GC:(g + 1) * GC]
        par[:, g, P_N:P_N + GC] = ng[:, g * GC:(g + 1) * GC]
    out["par"], out["halo_b"] = par, halo_b
    out["halo_a"] = a["state_conv_a"][0].reshape(NB, HA, KM, P).transpose(2, 3, 0, 1)
    out["dt_bias"], out["a_log"] = a["dt_bias"][0], a["a_log"][0]
    out["h_sample"] = a["state_ssm"][0].reshape(NB, G, HG * PD, NS).transpose(1, 0, 3, 2)
    i = np.arange(P)
    causal, same = i[:, None] <= i[None, :], i[:, None] // TS == i[None, :] // TS
    out["const"] = np.stack([causal, causal & same, np.ones((P, P), bool), same, i[:, None] == i[None, :]], 1
                            ).astype(np.float32)
    out["bmask"] = (i[:, None] // TS == np.arange(NB)[None, :]).astype(np.float32)
    return {k: np.ascontiguousarray(out[k]) for k in NAMES}


def bring_back(r):
    import numpy as np

    y = r["y"].reshape(DM, T).T
    na_p = r["new_a_prompt"].transpose(2, 0, 1).reshape(1, 1, HA, DM)
    na_s = r["new_a_sample"].transpose(2, 3, 0, 1).reshape(1, NB, HA, DM)
    nb = r["new_b"]
    nb = np.concatenate([nb[:, :, :GC].reshape(P, G * GC, -1), nb[:, :, GC], nb[:, :, GC + 1]], 1)
    nb = nb.transpose(2, 1, 0).reshape(HB + NB * HB, -1)
    hp = r["new_h_prompt"].transpose(0, 2, 1).reshape(1, 1, H, PD, NS)
    hs = r["new_h_sample"].transpose(1, 0, 3, 2).reshape(1, NB, H, PD, NS)
    outs = (y[:TP].reshape(1, TP, DM), y[TP:].reshape(NB, TS, DM), na_p, nb[:HB].reshape(1, 1, HB, -1), hp,
            na_s, nb[HB:].reshape(1, NB, HB, -1), hs)
    return tuple(np.ascontiguousarray(o) for o in outs)


def kernel(**inputs):
    import concourse.bacc as _bacc
    from concourse.bass_utils import run_bass_kernel_spmd as _run

    nc = _bacc.Bacc("TRN2", target_bir_lowering=False, num_devices=1)
    laid = lay_out(inputs)
    d = {n: nc.dram_tensor(f"in_{n}", a.shape, mybir.dt.from_np(a.dtype), kind="ExternalInput").ap()
         for n, a in laid.items()}
    for n, shape in OUTS.items():
        d[n] = nc.dram_tensor(f"out_{n}", shape, F32, kind="ExternalOutput").ap()
    build(nc, d)
    r = _run(nc, [{f"in_{n}": a for n, a in laid.items()}], core_ids=[0])
    return bring_back({n: r.results[0][f"out_{n}"] for n in OUTS})
```
